# Optimizing a Trainium2 kernel written in Bass

```python
import functools
import jax
import jax.numpy as jnp
from jax import lax
import numpy as np

D_MODEL = 1024
BATCH = 1
SEQ = 1024
DEPTH = 1
DEC_BATCH = 8
DEC_SEQ = 4
PAST_LEN = 4096
PAGE_SIZE = 128

GDN_HEADS = 8
GDN_HEAD_DIM = 128
GDN_DIM = GDN_HEADS * GDN_HEAD_DIM
GDN_QKV_DIM = 3 * GDN_DIM
CONV_WIDTH = 4
GDN_CHUNK = 64
NSA_HEADS = 8
NSA_KV_HEADS = 2
NSA_GROUP = NSA_HEADS // NSA_KV_HEADS
NSA_HEAD_DIM = 64
NSA_DIM = NSA_HEADS * NSA_HEAD_DIM
NSA_KV_DIM = NSA_KV_HEADS * NSA_HEAD_DIM
CMP_STRIDE = 16
CMP_LEN = 2 * CMP_STRIDE
SEL_BLOCK = 64
SEL_RATIO = SEL_BLOCK // CMP_STRIDE
N_SELECT = 16
WINDOW = 512
NSA_QBLOCK = 16
FORCE_BONUS = 100.0
IN_SPLITS = (GDN_QKV_DIM, GDN_HEADS, GDN_HEADS, GDN_DIM, NSA_DIM, 6 * NSA_KV_DIM, 3 * NSA_HEADS, NSA_DIM, 2 * D_MODEL)
IN_DIM = GDN_QKV_DIM + 2 * GDN_HEADS + GDN_DIM + 2 * NSA_DIM + 6 * NSA_KV_DIM + 3 * NSA_HEADS + 2 * D_MODEL
RMS_EPS = 1e-6
NEG_INF = -1e30

kernel_name = 'gdn_nsa_parallel_hybrid_step'

def rmsnorm(x, gain):
    xf = x.astype(jnp.float32)
    y = xf * lax.rsqrt(jnp.mean(xf * xf, axis=-1, keepdims=True) + RMS_EPS)
    return (y * gain.astype(jnp.float32)).astype(x.dtype)

def l2norm(x):
    xf = x.astype(jnp.float32)
    return xf * lax.rsqrt(jnp.sum(xf * xf, axis=-1, keepdims=True) + 1e-6)

def masked_softmax(s, mask):
    s = jnp.where(mask, s.astype(jnp.float32), NEG_INF)
    e = jnp.where(mask, jnp.exp(s - jnp.max(s, axis=-1, keepdims=True)), 0.0)
    return e / jnp.maximum(jnp.sum(e, axis=-1, keepdims=True), 1e-30)

def causal_conv_silu(xp, w):
    t = xp.shape[1] - CONV_WIDTH + 1
    y = sum(xp[:, j:j + t] * w[j] for j in range(CONV_WIDTH))
    return jax.nn.silu(y)

def gated_delta_chunked(q, k, v, g, beta, s0):
    b, t, h, dk = q.shape
    dv = v.shape[-1]
    c = min(GDN_CHUNK, t)
    pad = (-t) % c
    n = (t + pad) // c

    def blocks(a):
        a = jnp.pad(a, [(0, 0), (0, pad)] + [(0, 0)] * (a.ndim - 2))
        return jnp.moveaxis(a.reshape((b, n, c) + a.shape[2:]), 3, 1)

    q, k, v, g, beta = (blocks(a) for a in (q, k, v, g, beta))
    gc = jnp.cumsum(g, axis=-1)
    causal = jnp.tril(jnp.ones((c, c), dtype=bool))
    strict = jnp.tril(jnp.ones((c, c), dtype=bool), -1)
    decay = jnp.exp(jnp.where(causal, gc[..., :, None] - gc[..., None, :], -jnp.inf))
    a_mat = jnp.where(strict, beta[..., :, None] * jnp.einsum('bhnid,bhnjd->bhnij', k, k) * decay, 0.0)
    rhs = jnp.concatenate([v * beta[..., None], k * (beta * jnp.exp(gc))[..., None]], axis=-1)
    sol = lax.linalg.triangular_solve(a_mat + jnp.eye(c, dtype=a_mat.dtype), rhs,
                                      left_side=True, lower=True, unit_diagonal=True)
    u, w = sol[..., :dv], sol[..., dv:]
    attn = jnp.einsum('bhnid,bhnjd->bhnij', q, k) * decay
    q_dec = q * jnp.exp(gc)[..., None]
    k_dec = k * jnp.exp(gc[..., -1:] - gc)[..., None]
    last = jnp.exp(gc[..., -1])

    def step(s, xs):
        u_c, w_c, a_c, qd_c, kd_c, l_c = xs
        v_new = u_c - jnp.einsum('bhck,bhkv->bhcv', w_c, s)
        o_c = jnp.einsum('bhck,bhkv->bhcv', qd_c, s) + jnp.einsum('bhij,bhjv->bhiv', a_c, v_new)
        s = s * l_c[..., None, None] + jnp.einsum('bhck,bhcv->bhkv', kd_c, v_new)
        return s, o_c

    xs = tuple(jnp.moveaxis(a, 2, 0) for a in (u, w, attn, q_dec, k_dec, last))
    s_fin, o = lax.scan(step, s0, xs)
    o = jnp.moveaxis(jnp.moveaxis(o, 0, 2), 1, 3).reshape(b, n * c, h, dv)[:, :t]
    return o, s_fin

def gdn_branch(qkv_p, a, bt, z, s0, conv_w, a_log, dt_bias, head_gain):
    qkv = causal_conv_silu(qkv_p, conv_w)
    b, t, _ = qkv.shape
    shp = (b, t, GDN_HEADS, GDN_HEAD_DIM)
    q, k, v = jnp.split(qkv, 3, axis=-1)
    q = l2norm(q.reshape(shp)) * GDN_HEAD_DIM ** -0.5
    k = l2norm(k.reshape(shp))
    v = v.reshape(shp).astype(jnp.float32)
    g = -jnp.exp(a_log.astype(jnp.float32)) * jax.nn.softplus(a.astype(jnp.float32) + dt_bias.astype(jnp.float32))
    beta = jax.nn.sigmoid(bt.astype(jnp.float32))
    o, s_new = gated_delta_chunked(q, k, v, g, beta, s0.astype(jnp.float32))
    o = rmsnorm(o, head_gain) * jax.nn.silu(z.astype(jnp.float32)).reshape(shp)
    return o.reshape(b, t, GDN_DIM), s_new

def compress(kv, pos_w, lin_w):
    b, l = kv.shape[:2]
    m = l // CMP_STRIDE
    ch = kv[:, :m * CMP_STRIDE].reshape(b, m, CMP_STRIDE, NSA_KV_HEADS, NSA_HEAD_DIM)
    lo = jnp.einsum('bmjgd,jd->bmgd', ch, pos_w[:CMP_STRIDE])
    hi = jnp.einsum('bmjgd,jd->bmgd', ch, pos_w[CMP_STRIDE:])
    return jnp.einsum('bmgd,de->bmge', lo[:, :-1] + hi[:, 1:], lin_w)

def nsa_attend(q, pos_q, kc, vc, gather_sel, n_blocks, kw, vw, pos_w, gates):
    b, tq = q.shape[:2]
    qg = q.reshape(b, tq, NSA_KV_HEADS, NSA_GROUP, NSA_HEAD_DIM) * NSA_HEAD_DIM ** -0.5
    nc = kc.shape[1]
    c_end = jnp.arange(nc) * CMP_STRIDE + CMP_LEN - 1
    mask_c = (c_end[None, :] <= pos_q[:, None])[None, :, None, None, :]
    p_c = masked_softmax(jnp.einsum('bqghd,bcgd->bqghc', qg, kc), mask_c)
    o_c = jnp.einsum('bqghc,bcgd->bqghd', p_c, vc)
    imp = jnp.pad(p_c.sum(axis=3), ((0, 0), (0, 0), (0, 0), (0, n_blocks * SEL_RATIO - nc)))
    imp = imp.reshape(b, tq, NSA_KV_HEADS, n_blocks, SEL_RATIO).sum(axis=-1)
    blk = jnp.arange(n_blocks)[None, :]
    cur = pos_q[:, None] // SEL_BLOCK
    valid = blk * SEL_BLOCK <= pos_q[:, None]
    forced = (blk == 0) | (blk == cur) | (blk == cur - 1)
    score = jnp.where(valid[None, :, None, :], imp + FORCE_BONUS * forced[None, :, None, :], -1.0)
    _, idx = lax.top_k(score, min(N_SELECT, n_blocks))
    n_sel = idx.shape[-1]
    k_s, v_s = gather_sel(idx)
    k_s = k_s.reshape(b, tq, NSA_KV_HEADS, n_sel * SEL_BLOCK, NSA_HEAD_DIM)
    v_s = v_s.reshape(b, tq, NSA_KV_HEADS, n_sel * SEL_BLOCK, NSA_HEAD_DIM)
    k_pos = (idx[..., None] * SEL_BLOCK + jnp.arange(SEL_BLOCK)).reshape(b, tq, NSA_KV_HEADS, 1, n_sel * SEL_BLOCK)
    mask_s = k_pos <= pos_q[None, :, None, None, None]
    p_s = masked_softmax(jnp.einsum('bqghd,bqgmd->bqghm', qg, k_s), mask_s)
    o_s = jnp.einsum('bqghm,bqgmd->bqghd', p_s, v_s)
    dist = pos_q[:, None] - pos_w[None, :]
    mask_w = ((dist >= 0) & (dist <= WINDOW) & (pos_w[None, :] >= 0))[None, :, None, None, :]
    p_w = masked_softmax(jnp.einsum('bqghd,bkgd->bqghk', qg, kw), mask_w)
    o_w = jnp.einsum('bqghk,bkgd->bqghd', p_w, vw)
    gt = gates.reshape(b, tq, NSA_KV_HEADS, NSA_GROUP, 3)
    o = gt[..., 0:1] * o_c + gt[..., 1:2] * o_s + gt[..., 2:3] * o_w
    return o.reshape(b, tq, NSA_DIM)

def nsa_prompt(q, gates, k_cmp, v_cmp, k_slc, v_slc, k_win, v_win, pos_k, w_k, pos_v, w_v):
    b, t = q.shape[:2]
    kc = compress(k_cmp, pos_k, w_k)
    vc = compress(v_cmp, pos_v, w_v)
    n_blocks = t // SEL_BLOCK
    kb = k_slc.reshape(b, n_blocks, SEL_BLOCK, NSA_KV_HEADS, NSA_HEAD_DIM)
    vb = v_slc.reshape(b, n_blocks, SEL_BLOCK, NSA_KV_HEADS, NSA_HEAD_DIM)
    b_ix = jnp.arange(b)[:, None, None, None]
    g_ix = jnp.arange(NSA_KV_HEADS)[None, None, :, None]

    def gather_sel(idx):
        return kb[b_ix, idx, :, g_ix, :], vb[b_ix, idx, :, g_ix, :]

    span = WINDOW + NSA_QBLOCK
    kw_pad = jnp.pad(k_win, ((0, 0), (WINDOW, 0), (0, 0), (0, 0)))
    vw_pad = jnp.pad(v_win, ((0, 0), (WINDOW, 0), (0, 0), (0, 0)))
    nqb = t // NSA_QBLOCK
    qb = q.reshape(b, nqb, NSA_QBLOCK, NSA_DIM).swapaxes(0, 1)
    gb = gates.reshape(b, nqb, NSA_QBLOCK, 3 * NSA_HEADS).swapaxes(0, 1)

    def one_block(args):
        q_blk, g_blk, q0 = args
        pos_q = q0 + jnp.arange(NSA_QBLOCK, dtype=jnp.int32)
        kw = lax.dynamic_slice_in_dim(kw_pad, q0, span, axis=1)
        vw = lax.dynamic_slice_in_dim(vw_pad, q0, span, axis=1)
        pos_w = q0 - WINDOW + jnp.arange(span, dtype=jnp.int32)
        return nsa_attend(q_blk, pos_q, kc, vc, gather_sel, n_blocks, kw, vw, pos_w, g_blk)

    o = lax.map(one_block, (qb, gb, jnp.arange(nqb, dtype=jnp.int32) * NSA_QBLOCK))
    keep = min(WINDOW, t)
    return o.swapaxes(0, 1).reshape(b, t, NSA_DIM), (k_win[:, t - keep:], v_win[:, t - keep:])

def nsa_sample(q, gates, k_cmp, v_cmp, k_slc, v_slc, k_win, v_win,
               pool_k_cmp, pool_v_cmp, pool_k_slc, pool_v_slc, buf_k_win, buf_v_win, page_table,
               pos_k, w_k, pos_v, w_v):
    b, t = q.shape[:2]
    n_pages = page_table.shape[1]
    page = pool_k_cmp.shape[1]
    past = n_pages * page
    pos_q = past + jnp.arange(t, dtype=jnp.int32)

    def past_rows(pool):
        return pool[page_table].reshape(b, past, NSA_KV_HEADS, NSA_HEAD_DIM)

    kc = compress(jnp.concatenate([past_rows(pool_k_cmp), k_cmp.astype(pool_k_cmp.dtype)], axis=1), pos_k, w_k)
    vc = compress(jnp.concatenate([past_rows(pool_v_cmp), v_cmp.astype(pool_v_cmp.dtype)], axis=1), pos_v, w_v)
    n_blocks = -(-(past + t) // SEL_BLOCK)
    past_blocks = past // SEL_BLOCK
    per_page = page // SEL_BLOCK
    new_blocks = n_blocks - past_blocks
    pad_new = new_blocks * SEL_BLOCK - t
    kn = jnp.pad(k_slc, ((0, 0), (0, pad_new), (0, 0), (0, 0))).reshape(b, new_blocks, SEL_BLOCK, NSA_KV_HEADS, NSA_HEAD_DIM)
    vn = jnp.pad(v_slc, ((0, 0), (0, pad_new), (0, 0), (0, 0))).reshape(b, new_blocks, SEL_BLOCK, NSA_KV_HEADS, NSA_HEAD_DIM)
    kp = pool_k_slc.reshape(-1, SEL_BLOCK, NSA_KV_HEADS, NSA_HEAD_DIM)
    vp = pool_v_slc.reshape(-1, SEL_BLOCK, NSA_KV_HEADS, NSA_HEAD_DIM)
    b_ix = jnp.arange(b)[:, None, None, None]
    g_ix = jnp.arange(NSA_KV_HEADS)[None, None, :, None]

    def gather_sel(idx):
        is_past = (idx < past_blocks)[..., None, None]
        ip = jnp.minimum(idx, past_blocks - 1)
        phys = page_table[b_ix, ip // per_page] * per_page + ip % per_page
        inew = jnp.clip(idx - past_blocks, 0, new_blocks - 1)
        k_sel = jnp.where(is_past, kp[phys, :, g_ix, :], kn[b_ix, inew, :, g_ix, :].astype(kp.dtype))
        v_sel = jnp.where(is_past, vp[phys, :, g_ix, :], vn[b_ix, inew, :, g_ix, :].astype(vp.dtype))
        return k_sel, v_sel

    w_buf = buf_k_win.shape[1]
    kw = jnp.concatenate([buf_k_win, k_win.astype(buf_k_win.dtype)], axis=1)
    vw = jnp.concatenate([buf_v_win, v_win.astype(buf_v_win.dtype)], axis=1)
    pos_w = past - w_buf + jnp.arange(w_buf + t, dtype=jnp.int32)
    o = nsa_attend(q, pos_q, kc, vc, gather_sel, n_blocks, kw, vw, pos_w, gates)
    keep = min(WINDOW, w_buf + t)
    return o, (kw[:, w_buf + t - keep:], vw[:, w_buf + t - keep:])

def layer(x, conv_prefix, s0, nsa_fn, norm_gain, w_in, conv_w, a_log, dt_bias, gdn_gain,
          w_branch_a, w_branch_b, w_out):
    b, t, _ = x.shape
    h = rmsnorm(x, norm_gain)
    bounds = np.cumsum(IN_SPLITS)[:-1].tolist()
    qkv, a, bt, z_a, q_b, kv_b, g_b, z_b, merge = jnp.split(jnp.einsum('btd,de->bte', h, w_in), bounds, axis=-1)
    qkv_p = jnp.concatenate([conv_prefix.astype(qkv.dtype), qkv], axis=1)
    o_a, s_new = gdn_branch(qkv_p, a, bt, z_a, s0, conv_w, a_log, dt_bias, gdn_gain)
    kvs = [r.reshape(b, t, NSA_KV_HEADS, NSA_HEAD_DIM) for r in jnp.split(kv_b, 6, axis=-1)]
    o_nsa, win_state = nsa_fn(q_b, jax.nn.sigmoid(g_b.astype(jnp.float32)), *kvs)
    o_b = o_nsa * jax.nn.silu(z_b.astype(jnp.float32))
    gate_a, gate_b = jnp.split(jax.nn.sigmoid(merge.astype(jnp.float32)), 2, axis=-1)
    mixed = (gate_a * jnp.einsum('bte,ed->btd', o_a, w_branch_a)
             + gate_b * jnp.einsum('bte,ed->btd', o_b, w_branch_b))
    x_new = x + jnp.einsum('btd,de->bte', mixed, w_out).astype(x.dtype)
    new_state = (kvs[0], kvs[1], kvs[2], kvs[3], win_state[0], win_state[1],
                 qkv_p[:, -(CONV_WIDTH - 1):], s_new)
    return x_new, new_state

def setup_inputs(seed: int = 0) -> dict:
    key = jax.random.key(seed)
    ks = jax.random.split(key, 32)
    f32 = jnp.float32
    n_pages = PAST_LEN // PAGE_SIZE
    n_pool = (DEC_BATCH * n_pages * 5) // 4
    w_buf = min(WINDOW, PAST_LEN)

    def nrm(k, shape, scale):
        return jax.random.normal(k, shape, f32) * scale

    pool_shape = (DEPTH, n_pool, PAGE_SIZE, NSA_KV_HEADS, NSA_HEAD_DIM)
    win_shape = (DEPTH, DEC_BATCH, w_buf, NSA_KV_HEADS, NSA_HEAD_DIM)
    perm = jax.random.permutation(ks[10], n_pool)[:DEC_BATCH * n_pages]
    page_table = perm.reshape(DEC_BATCH, n_pages).astype(jnp.int32)
    return {
        'x_prompt': nrm(ks[0], (BATCH, SEQ, D_MODEL), 1.0),
        'x_sample': nrm(ks[1], (DEC_BATCH, DEC_SEQ, D_MODEL), 1.0),
        'cache_k_cmp': nrm(ks[2], pool_shape, 1.0),
        'cache_v_cmp': nrm(ks[3], pool_shape, 1.0),
        'cache_k_slc': nrm(ks[4], pool_shape, 1.0),
        'cache_v_slc': nrm(ks[5], pool_shape, 1.0),
        'state_win_k': nrm(ks[6], win_shape, 1.0),
        'state_win_v': nrm(ks[7], win_shape, 1.0),
        'state_conv': nrm(ks[8], (DEPTH, DEC_BATCH, CONV_WIDTH - 1, GDN_QKV_DIM), 1.0),
        'state_gdn': nrm(ks[9], (DEPTH, DEC_BATCH, GDN_HEADS, GDN_HEAD_DIM, GDN_HEAD_DIM), 0.5),
        'page_table': page_table,
        'norm_gain': 1.0 + nrm(ks[11], (DEPTH, D_MODEL), 0.02),
        'w_in': nrm(ks[12], (DEPTH, D_MODEL, IN_DIM), D_MODEL ** -0.5),
        'conv_w': nrm(ks[13], (DEPTH, CONV_WIDTH, GDN_QKV_DIM), CONV_WIDTH ** -0.5),
        'a_log': jnp.log(jax.random.uniform(ks[14], (DEPTH, GDN_HEADS), f32, 1.0, 16.0)),
        'dt_bias': nrm(ks[15], (DEPTH, GDN_HEADS), 0.1),
        'gdn_gain': 1.0 + nrm(ks[16], (DEPTH, GDN_HEAD_DIM), 0.02),
        'cmp_pos_k': (1.0 + nrm(ks[17], (DEPTH, CMP_LEN, NSA_HEAD_DIM), 0.1)) * CMP_LEN ** -0.5,
        'cmp_w_k': nrm(ks[18], (DEPTH, NSA_HEAD_DIM, NSA_HEAD_DIM), NSA_HEAD_DIM ** -0.5),
        'cmp_pos_v': (1.0 + nrm(ks[19], (DEPTH, CMP_LEN, NSA_HEAD_DIM), 0.1)) * CMP_LEN ** -0.5,
        'cmp_w_v': nrm(ks[20], (DEPTH, NSA_HEAD_DIM, NSA_HEAD_DIM), NSA_HEAD_DIM ** -0.5),
        'w_branch_a': nrm(ks[21], (DEPTH, GDN_DIM, D_MODEL), GDN_DIM ** -0.5),
        'w_branch_b': nrm(ks[22], (DEPTH, NSA_DIM, D_MODEL), NSA_DIM ** -0.5),
        'w_out': nrm(ks[23], (DEPTH, D_MODEL, D_MODEL), D_MODEL ** -0.5),
        'final_gain': 1.0 + nrm(ks[24], (D_MODEL,), 0.02),
    }

def reference(x_prompt, x_sample, cache_k_cmp, cache_v_cmp, cache_k_slc, cache_v_slc,
              state_win_k, state_win_v, state_conv, state_gdn, page_table,
              norm_gain, w_in, conv_w, a_log, dt_bias, gdn_gain,
              cmp_pos_k, cmp_w_k, cmp_pos_v, cmp_w_v,
              w_branch_a, w_branch_b, w_out, final_gain):
    hp, hs = x_prompt, x_sample
    bp = x_prompt.shape[0]
    prompt_states, sample_states = [], []
    for l in range(DEPTH):
        lw = (norm_gain[l], w_in[l], conv_w[l], a_log[l], dt_bias[l], gdn_gain[l],
              w_branch_a[l], w_branch_b[l], w_out[l])
        cmp_p = dict(pos_k=cmp_pos_k[l], w_k=cmp_w_k[l], pos_v=cmp_pos_v[l], w_v=cmp_w_v[l])
        nsa_p = functools.partial(nsa_prompt, **cmp_p)
        nsa_s = functools.partial(nsa_sample, pool_k_cmp=cache_k_cmp[l], pool_v_cmp=cache_v_cmp[l],
                                  pool_k_slc=cache_k_slc[l], pool_v_slc=cache_v_slc[l],
                                  buf_k_win=state_win_k[l], buf_v_win=state_win_v[l],
                                  page_table=page_table, **cmp_p)
        conv0 = jnp.zeros((bp, CONV_WIDTH - 1, GDN_QKV_DIM), hp.dtype)
        gdn0 = jnp.zeros((bp, GDN_HEADS, GDN_HEAD_DIM, GDN_HEAD_DIM), jnp.float32)
        hp, st_p = layer(hp, conv0, gdn0, nsa_p, *lw)
        hs, st_s = layer(hs, state_conv[l], state_gdn[l], nsa_s, *lw)
        prompt_states.append(st_p)
        sample_states.append(st_s)
    y_prompt = rmsnorm(hp, final_gain)
    y_sample = rmsnorm(hs, final_gain)
    (k_cmp_p, v_cmp_p, k_slc_p, v_slc_p, win_k_p, win_v_p, conv_p, gdn_p) = [jnp.stack(z) for z in zip(*prompt_states)]
    (k_cmp_s, v_cmp_s, k_slc_s, v_slc_s, win_k_s, win_v_s, conv_s, gdn_s) = [jnp.stack(z) for z in zip(*sample_states)]
    return (y_prompt, y_sample,
            k_cmp_p, v_cmp_p, k_slc_p, v_slc_p, win_k_p, win_v_p, conv_p, gdn_p,
            k_cmp_s, v_cmp_s, k_slc_s, v_slc_s, win_k_s, win_v_s, conv_s, gdn_s)


_drawn_inputs = setup_inputs


def setup_inputs(seed=0):
    import zlib

    import numpy as np

    out = dict(_drawn_inputs(seed))
    spreads = {}
    factors = {'cache_k_cmp': 3.116,
     'cache_k_slc': 8.0,
     'cache_v_slc': 6.367,
     'dt_bias': 2.942,
     'gdn_gain': 8.0,
     'cmp_pos_k': 8.0,
     'cmp_pos_v': 8.0,
     'final_gain': 2.856}
    for name, (base, spread) in spreads.items():
        noise = np.random.default_rng([zlib.crc32(name.encode()), seed]).standard_normal(out[name].shape)
        drawn = base * np.exp(spread * noise) if base else spread * noise
        out[name] = jnp.asarray(drawn.astype(out[name].dtype))
    for name, factor in factors.items():
        out[name] = (out[name] * factor).astype(out[name].dtype)
    return out
```

```python
from contextlib import ExitStack

import concourse.bass as bass
import numpy as np
from concourse import mybir

F32 = mybir.dt.float32
I32 = mybir.dt.int32
U32 = mybir.dt.uint32
ALU = mybir.AluOpType
ACT = mybir.ActivationFunctionType
AX = mybir.AxisListType.X
ds = bass.ds

P = 128
D = 1024
KT = D // P
SEQ = 1024
PT = SEQ // P
NB, NS = 8, 4
SAMPLE = NB * NS
T = SEQ + SAMPLE
TT = PT + 1
TP = TT * P
CHUNKS = [(0, 512), (512, 512), (1024, SAMPLE)]
THIRDS = [(n * T // 3, T // 3) for n in range(3)]
HEADS, DH = 8, 128
PAIRS, DN = 4, 64
PAST, PAGE = 4096, 128
PAGES = PAST // PAGE
CONV = 4
CS, CL = 16, 32
NCB = SEQ // CS - 1
NCS = PAST // CS - 1
SB = 64
NBLK = PAST // SB + 1
TOP = 16
WIN = 512
EPS = 1e-6
BIG = 1e30
C_A, C_B, C_Z, C_Q, C_KV, C_G, C_ZB, C_M = 3072, 3080, 3088, 4112, 4624, 5392, 5416, 5928
LEVELS = [1, 2, 4, 8, 16, 32, 64]


def const_parts():
    j = np.arange(P)[:, None]
    i = np.arange(P)[None, :]
    same4 = (j // NS == i // NS)
    c = {}
    c["ident"] = (j == i)
    c["ones"] = np.ones((P, P))
    c["cum"] = np.stack([j <= i, (j <= i) & same4], 1)
    c["tot4"] = same4
    c["upper"] = np.where(c["cum"], 0.0, -BIG)
    c["lower"] = np.where(np.stack([j > i, (j > i) & same4], 1), 0.0, BIG)
    c["level"] = np.stack([-1.0 * ((j // (2 * s) == i // (2 * s)) & (i % (2 * s) >= s) & (j % (2 * s) < s))
                           for s in LEVELS], 1)
    c["seqcol"] = (np.arange(NB)[None, :, None] == np.arange(SAMPLE)[None, None, :] // NS) * np.ones((P, 1, 1))
    c["seqany"] = (j < SAMPLE)
    c["seqrow"] = (np.arange(P)[:, None] // NS == np.arange(NB)[None, :])
    return {k: np.asarray(v, np.float32) for k, v in c.items()}


def nsa_parts():
    c = {}
    p = np.arange(P)
    q, k = p[:, None], p[None, :]
    c["causal"] = np.where(k <= q, 0.0, -BIG)
    c["edge"] = np.where(k >= q, 0.0, -BIG)
    blk = np.arange(NCB)[None, None, :]
    tok = (np.arange(PT)[None, :, None] * P + p[:, None, None])
    c["seen"] = (blk * CS + CL - 1 <= tok)
    c["unseen"] = np.where(c["seen"], 0.0, -BIG)
    return {k_: np.asarray(v, np.float32) for k_, v in c.items()}


def row_parts():
    c = {}
    R = 64
    row = np.arange(R)
    g, h, t, used = row // 32, row % 32 // NS, row % NS, row % 32 < 16
    out = np.arange(R)
    ob, og, ot = out // 8, out // 4 % 2, out % 4
    b = np.arange(NB)
    c["heads_in"] = (used[:, None, None] & (g[:, None, None] == og) & (t[:, None, None] == ot)
                     & (b[None, :, None] == ob))
    c["heads_out"] = c["heads_in"].transpose(2, 1, 0)
    key = np.arange(SAMPLE)
    c["new"] = np.where((key // NS == b[None, :, None]) & (key % NS <= t[:, None, None]), 0.0, -BIG)
    s, kp = np.arange(4)[:, None], np.arange(P)[None, :]
    c["win"] = np.where((kp * 4 + s)[None] >= t[:, None, None], 0.0, -BIG)
    c["tok_row"] = ((key[:, None, None] // NS == b[None, :, None]) & (key[:, None, None] % NS == t))
    gh = np.arange(8)
    c["pick"] = (used[:, None] & (gh // 4 == g[:, None]) & (gh % 4 == h[:, None]))
    c["own"] = (g[:, None] == np.arange(P)[None, :] // DN)
    c["force"] = np.tile(np.isin(np.arange(NBLK), (0, NBLK - 2, NBLK - 1)) * 100.0, (R, 1))
    c["mod8"] = (np.arange(P) % 8)[:, None]
    c["before"] = np.tile((np.arange(NBLK)[None, :] < np.arange(NBLK)[:, None])[None], (R, 1, 1))
    return {k: np.pad(np.asarray(v, np.float32), [(0, P - len(v))] + [(0, 0)] * (v.ndim - 1)) for k, v in c.items()}


def pack(parts):
    return np.concatenate([v.reshape(P, -1) for v in parts.values()], 1)


class Packed:

    def __init__(self, tile, parts):
        self.at, off = {}, 0
        for k, v in parts.items():
            n = v.size // P
            ap = tile[:, off:off + n]
            if v.ndim == 3:
                ap = ap.rearrange("p (a b) -> p a b", a=v.shape[1])
            self.at[k] = ap
            off += n

    def __getitem__(self, k):
        return self.at[k]


class Turn:
    def __init__(self, bank, free, full, done):
        self.bank, self.free, self.full, self.done = bank, free, full, done


class Ring:

    def __init__(self, banks, names):
        self.banks, self.names, self.n = banks, names, len(names)
        self.order = {k: n for n, k in enumerate(names)}
        assert len(self.order) == self.n

    def at(self, name, i=0):
        k, r = self.order[name], len(self.banks)
        free = k + 1 if self.n % r == 0 or k >= r else r
        return Turn(self.banks[k % r], i * self.n + free, i * self.n + k + 1, i * self.n + k + 1 + r)


class Count:

    def __init__(self, i=0, per=0):
        self.i, self.per, self.k = i, per, 0

    def next(self):
        self.k += 1
        return self.i * self.per + self.k if self.per else self.k

    def end(self):
        assert not self.per or self.k == self.per, f"per={self.k}"


def rep(ap, axis, n):
    shape = list(ap.shape)
    return ap.unsqueeze(axis).to_broadcast(shape[:axis] + [n] + shape[axis:])


def stage_norm(nc, g, x_prompt, x_sample, norm_gain, w_in, conv_w, a_log, dt_bias):
    c, hT, SC, DEC, gates, beta = g.c, g.hT, g.SC, g.DEC, g.gates, g.beta
    w_rows = w_in[0].rearrange("(k p) n -> p k n", p=P)
    with ExitStack() as ctx:
        def sb(name, shape, dt=F32):
            return ctx.enter_context(nc.sbuf_tensor("n_" + name, shape, dt))

        def sem(name):
            return ctx.enter_context(nc.semaphore("n_" + name))

        x = sb("x", [P, TT, D])
        sq = sb("sq", [P, 2, D])
        ss = sb("ss", [P, TT])
        rstd = sb("rstd", [P, TT])
        half = sb("half", [P, TT])
        gain = sb("gain", [P, KT])
        gain_rows = sb("gain_rows", [KT, P])
        cw_rows = sb("cw_rows", [CONV * 3 * HEADS, P])
        ws = sb("ws", [P, KT, 40])
        small = sb("small", [40, T])
        tok = sb("tok", [P, TT, 40])
        al = sb("al", [P, HEADS])
        dtb = sb("dtb", [P, HEADS])
        z = sb("z", [P, TT, HEADS])
        za = sb("za", [P, TT, HEADS])
        ga = sb("ga", [P, TT, HEADS])
        gseq = sb("gseq", [SAMPLE, NB, HEADS])
        gc = sb("gc", [P, TT, HEADS])
        gl = sb("gl", [P, TT, HEADS])
        th = sb("th", [P, TT, 32])
        ps = ctx.enter_context(nc.psum_tensor("n_ps", [P, 8, 512], F32))

        x_loaded = [sem(f"x_loaded{i}") for i in range(TT)]
        c_loaded, g_loaded, ws_loaded, cw_loaded, i_loaded = sem("c_loaded"), sem("g_loaded"), sem("ws_loaded"), sem("cw_loaded"), sem("i_loaded")
        al_loaded, dt_loaded = sem("al_loaded"), sem("dt_loaded")
        squared, rooted, scaled = sem("squared"), sem("rooted"), sem("scaled")
        filled, emptied = sem("filled"), sem("emptied")
        a_step, v_step, p_step = sem("a_step"), sem("v_step"), sem("p_step")
        v_to_act, act_to_v, v_to_pe = sem("v_to_act"), sem("act_to_v"), sem("v_to_pe")

        halves = [f"x{t}{s}" for t in range(TT) for s in range(2)]
        R = Ring([0, 1, 2, 3], ["gain", "cw"] + halves + ["s0", "s1", "s2", "tok", "cum"])
        def norm_out(v, t):
            n = P if t < PT else SAMPLE
            for s in range(2):
                k = R.at(f"x{t}{s}")
                v.wait_ge(filled, k.full)
                v.tensor_tensor(hT[:, 4 * s:4 * s + 4, t * P:t * P + n],
                                ps[:, k.bank, :].rearrange("p (q n) -> p q n", n=P)[:, :, 0:n],
                                rep(gain[:, 4 * s:4 * s + 4], 2, n), ALU.mult).then_inc(emptied, 1)

        block = ctx.enter_context(nc.Block())

        @block.sync
        def _(sp):
            for t in range(PT):
                sp.dma_start(x[:, t, :], x_prompt[0, t * P:(t + 1) * P, :]).then_inc(x_loaded[t], 16)
                if t == 0:
                    sp.dma_start(g.ctile[:], g.consts).then_inc(c_loaded, 16)
                    sp.dma_start(g.ident_tile[:], g.consts[:, 0:P]).then_inc(i_loaded, 16)
                    sp.dma_start(gain_rows[:], norm_gain.rearrange("a (k p) -> (a k) p", p=P)).then_inc(g_loaded, 16)
            sp.dma_start(cw_rows[:], conv_w[0].rearrange("j (r p) -> (j r) p", p=P)).then_inc(cw_loaded, 16)
            sp.dma_start(x[0:SAMPLE, PT, :], x_sample.rearrange("b s d -> (b s) d")).then_inc(x_loaded[PT], 16)
            sp.dma_start(ws[:, :, 0:16], w_rows[:, :, C_A:C_A + 16]).then_inc(ws_loaded, 16)
            sp.dma_start(ws[:, :, 16:40], w_rows[:, :, C_G:C_G + 24]).then_inc(ws_loaded, 16)
            sp.dma_start(al[:], a_log[0].partition_broadcast(P)).then_inc(al_loaded, 16)
            sp.dma_start(dtb[:], dt_bias[0].partition_broadcast(P)).then_inc(dt_loaded, 16)

        @block.gpsimd
        def _(gp):
            p = Count()

            def step(ins):
                ins.then_inc(p_step, 1)
                gp.wait_ge(p_step, p.next())

            step(gp.memset(half[:], -0.5))
            gp.wait_ge(squared, TT)
            step(gp.tensor_scalar(rstd[:], ss[:], 1.0 / D, EPS, ALU.mult, ALU.add))
            gp.tensor_tensor(rstd[:], rstd[:], half[:], ALU.pow).then_inc(rooted, 1)

        @block.scalar
        def _(act):
            a = Count()

            def step(ins):
                ins.then_inc(a_step, 1)
                act.wait_ge(a_step, a.next())

            act.wait_ge(v_to_act, 1)
            for t in range(TT):
                n = P if t < PT else SAMPLE
                act.wait_ge(x_loaded[t], 16)
                if t >= 2:
                    act.wait_ge(squared, t - 1)
                act.activation(sq[0:n, t % 2, :], x[0:n, t, :], ACT.Square,
                               accum_out=ss[0:n, t:t + 1]).then_inc(squared, 1)
            act.wait_ge(emptied, R.at("tok").done)
            act.activation(th[:], tok[:, :, 8:40], ACT.Tanh, scale=0.5).then_inc(act_to_v, 1)
            act.wait_ge(v_to_act, 2)
            step(act.activation(za[:], z[:], ACT.Abs))
            step(act.activation(za[:], za[:], ACT.Exp, scale=-1.0))
            act.activation(za[:], za[:], ACT.Ln, bias=1.0).then_inc(act_to_v, 1)
            act.wait_ge(al_loaded, 16)
            act.activation(al[:], al[:], ACT.Exp).then_inc(act_to_v, 1)
            act.wait_ge(v_to_act, 3)
            step(act.activation(SC[:, :, 2:4, :], SC[:, :, 2:4, :], ACT.Exp))
            act.activation(DEC[:], DEC[:], ACT.Exp).then_inc(act_to_v, 1)

        @block.tensor
        def _(pe):
            pe.wait_ge(c_loaded, 16)
            pe.wait_ge(g_loaded, 16)
            pe.wait_ge(i_loaded, 16)
            k = R.at("gain")
            pe.wait_ge(emptied, k.free)
            pe.transpose(ps[:, k.bank, 0:KT], gain_rows[:], c["ident"][0:KT, 0:KT]).then_inc(filled, 1)
            k = R.at("cw")
            pe.wait_ge(cw_loaded, 16)
            pe.transpose(ps[:, k.bank, 0:96], cw_rows[:], c["ident"][0:96, 0:96]).then_inc(filled, 1)
            for t in range(TT):
                n = P if t < PT else SAMPLE
                pe.wait_ge(scaled, t + 1)
                for s in range(2):
                    k = R.at(f"x{t}{s}")
                    pe.wait_ge(emptied, k.free)
                    for q in range(4):
                        kt = 4 * s + q
                        ins = pe.transpose(ps[:, k.bank, q * P:q * P + n], x[0:n, t, kt * P:(kt + 1) * P],
                                           c["ident"][0:n, 0:n])
                    ins.then_inc(filled, 1)
            pe.wait_ge(ws_loaded, 32)
            for s, (t0, n) in enumerate(CHUNKS):
                k = R.at(f"s{s}")
                pe.wait_ge(emptied, k.free)
                if s == 0:
                    pe.wait_ge(emptied, R.at(f"x{PT}1").done)
                for kt in range(KT):
                    ins = pe.matmul(ps[0:40, k.bank, 0:n], ws[:, kt, :], hT[:, kt, t0:t0 + n],
                                    start=kt == 0, stop=kt == KT - 1)
                ins.then_inc(filled, 1)
            k = R.at("tok")
            pe.wait_ge(emptied, R.at("s2").done)
            for t in range(TT):
                n = P if t < PT else SAMPLE
                ins = pe.transpose(ps[0:n, k.bank, t * 40:(t + 1) * 40], small[:, t * P:t * P + n],
                                   c["ident"][0:40, 0:40])
            ins.then_inc(filled, 1)
            k = R.at("cum")
            pe.wait_ge(emptied, k.free)
            pe.wait_ge(v_to_pe, 1)
            bank = ps[:, k.bank, :]
            flat = ga[:, 0:PT, :].rearrange("p t h -> p (t h)")
            pe.matmul(bank[:, 0:64], c["cum"][:, 0, :], flat, start=True, stop=True)
            pe.matmul(bank[:, 64:72], c["cum"][:, 1, :], ga[:, PT, :], start=True, stop=True)
            pe.matmul(bank[:, 128:192], c["ones"], flat, start=True, stop=True)
            pe.matmul(bank[:, 192:200], c["tot4"], ga[:, PT, :], start=True, stop=True)
            pe.matmul(bank[:, 256:320], c["ones"][0:SAMPLE, :], gseq[:, :, :].rearrange("p b h -> p (b h)"),
                      start=True, stop=True).then_inc(filled, 1)

        @block.vector
        def _(v):
            n_step = Count()

            def step(ins):
                ins.then_inc(v_step, 1)
                v.wait_ge(v_step, n_step.next())

            v.sem_inc(emptied, 4)
            v.memset(ss[:], 1.0).then_inc(v_to_act, 1)
            step(v.memset(tok[:, PT, :], 0.0))
            k = R.at("gain")
            v.wait_ge(filled, k.full)
            v.tensor_copy(gain[:], ps[:, k.bank, 0:KT]).then_inc(emptied, 1)
            k = R.at("cw")
            v.wait_ge(filled, k.full)
            v.tensor_scalar(g.taps[:].rearrange("p h c j -> p j c h"), ps[:, k.bank, 0:96].rearrange("p (j c h) -> p j c h", j=CONV, c=3),
                            0.5, None, ALU.mult).then_inc(emptied, 1)
            v.wait_ge(emptied, k.done)
            v.wait_ge(rooted, 1)
            for t in range(TT):
                n = P if t < PT else SAMPLE
                if t == 0:
                    v.wait_ge(squared, TT)
                v.wait_ge(x_loaded[t], 16)
                v.tensor_scalar(x[0:n, t, :], x[0:n, t, :], rstd[0:n, t:t + 1], None, ALU.mult).then_inc(scaled, 1)
                if t:
                    norm_out(v, t - 1)
            norm_out(v, TT - 1)
            for s, (t0, n) in enumerate(CHUNKS):
                k = R.at(f"s{s}")
                v.wait_ge(filled, k.full)
                v.tensor_copy(small[:, t0:t0 + n], ps[0:40, k.bank, 0:n]).then_inc(emptied, 1)
            k = R.at("tok")
            v.wait_ge(filled, k.full)
            step(v.tensor_copy(tok[:, 0:PT, :], ps[:, k.bank, 0:PT * 40].rearrange("p (t n) -> p t n", n=40)))
            v.tensor_copy(tok[0:SAMPLE, PT, :], ps[0:SAMPLE, k.bank, PT * 40:TT * 40]).then_inc(emptied, 1)
            v.wait_ge(emptied, k.done)
            v.wait_ge(dt_loaded, 16)
            v.tensor_tensor(z[:], tok[:, :, 0:8], rep(dtb[:, :], 1, TT), ALU.add).then_inc(v_to_act, 1)
            v.wait_ge(v_to_act, 2)
            v.wait_ge(act_to_v, 1)
            step(v.tensor_scalar(beta[:], th[:, :, 0:8], 0.5, 0.5, ALU.mult, ALU.add))
            step(v.tensor_scalar(gates[:], th[:, :, 8:32], 0.5, 0.5, ALU.mult, ALU.add))
            v.wait_ge(act_to_v, 2)
            step(v.scalar_tensor_tensor(ga[:], z[:], 0.0, za[:], ALU.max, ALU.add))
            v.wait_ge(act_to_v, 3)
            step(v.tensor_scalar(al[:], al[:], -1.0, None, ALU.mult))
            step(v.tensor_tensor(ga[:], ga[:], rep(al[:, :], 1, TT), ALU.mult))
            step(v.tensor_scalar(ga[:, PT, :], ga[:, PT, :], c["seqany"], None, ALU.mult))
            v.tensor_tensor(gseq[:], rep(ga[0:SAMPLE, PT, :], 1, NB), rep(c["seqrow"][0:SAMPLE, :], 2, HEADS),
                            ALU.mult).then_inc(v_to_pe, 1)
            k = R.at("cum")
            v.wait_ge(filled, k.full)
            bank = ps[:, k.bank, :]
            step(v.tensor_copy(gc[:].rearrange("p t h -> p (t h)"), bank[:, 0:72]))
            step(v.tensor_copy(gl[:].rearrange("p t h -> p (t h)"), bank[:, 128:200]))
            step(v.tensor_copy(DEC[:, :, 0:PT], bank[:, 128:192].rearrange("p (t h) -> p h t", h=HEADS)))
            v.tensor_copy(DEC[:, :, PT:2 * PT], bank[:, 256:320].rearrange("p (b h) -> p h b", h=HEADS)
                          ).then_inc(emptied, 1)
            v.wait_ge(emptied, k.done)
            gch, glh = gc[:].rearrange("p t h -> p h t"), gl[:].rearrange("p t h -> p h t")
            step(v.tensor_copy(SC[:, :, 0, :], gch))
            step(v.tensor_copy(SC[:, :, 1, :], beta[:].rearrange("p t h -> p h t")))
            step(v.tensor_copy(SC[:, :, 2, :], gch))
            step(v.tensor_copy(SC[:, :, 5, :], ga[:].rearrange("p t h -> p h t")))
            v.tensor_tensor(SC[:, :, 3, :], glh, gch, ALU.subtract).then_inc(v_to_act, 1)
            v.wait_ge(act_to_v, 4)
            step(v.tensor_tensor(SC[:, :, 4, :], SC[:, :, 1, :], SC[:, :, 2, :], ALU.mult))



def gdn_rings():
    u3, u2 = range(3), range(2)
    lev = [(n, u) for n in range(len(LEVELS)) for u in (u3 if LEVELS[n] < NS else u2)]
    proj = [f"{x}{s}" for x in "qkvz" for s in u3]
    act = [f"t{x}{u}" for x in "qkv" for u in u3] + [f"b{x}{u}" for x in "qdk" for u in u3]
    dve = ["pre", "tail"] + [f"{x}{u}" for x in ("G", "A", "Q") for u in u3]
    for n in range(len(LEVELS)):
        us = [u for m, u in lev if m == n]
        dve += [f"Y{n}{u}" for u in us]
        if n:
            act += [f"T{n}{u}" for u in us]
            dve += [f"U{n}{u}" for u in us]
    act += [f"W{u}" for u in u3]
    for t in range(PT):
        dve += [f"V{t}", f"S{t}"]
        act += [f"O{t}"]
    dve += ["V8", "S8a", "S8b"] + [f"N{u}" for u in u3]
    act += ["O8"]
    return proj, act, dve


def stage_gdn(nc, g, w_in, state_conv, state_gdn, gdn_gain, conv_p, conv_s, gdn_p, gdn_s):
    c, hT, oAT = g.c, g.hT, g.oAT
    w_rows = w_in[0].rearrange("(k p) n -> p k n", p=P)
    names_proj, names_act, names_dve = gdn_rings()
    RP, RA, RD = Ring([0, 1], names_proj), Ring([2, 3, 4], names_act), Ring([5, 6, 7], names_dve)
    tiles_of = [range(0, 4), range(4, 8), range(8, 9)]
    with ExitStack() as ctx:
        def sb(name, shape, dt=F32):
            return ctx.enter_context(nc.sbuf_tensor("g_" + name, shape, dt))

        def sem(name):
            return ctx.enter_context(nc.semaphore("g_" + name))

        W = sb("W", [P, 4, KT, P])
        XW = 3 + SEQ + NB * 7
        X3 = sb("X3", [P, 3, XW])
        r1 = sb("r1", [P, 3 * TP])
        r2 = sb("r2", [P, 3, TP])
        r3 = sb("r3", [P, 3 * TP])
        qnT, qdT, knT = (r1[:, n * TP:(n + 1) * TP] for n in range(3))
        Y3 = r2
        qn, kn, Rk = (r2[:, n, :].rearrange("p (t d) -> p t d", d=P) for n in range(3))
        T3 = r3[:, 0:3 * T].rearrange("p (c n) -> p c n", c=3)
        Tm, TTm, YT = (r3[:, n * TP:(n + 1) * TP].rearrange("p (t d) -> p t d", d=P) for n in range(3))
        zh = sb("zh", [P, T])
        tok = sb("tok", [P, 3, TT, P])
        EE = sb("EE", [P, 2, TT, P])
        sq = EE
        Elo, Eup = EE[:, 0, :, :], EE[:, 1, :, :]
        UG = sb("UG", [P, TT, P])
        Ot = UG
        Dm = sb("Dm", [P, TT, P])
        zt = Dm[:].rearrange("p t d -> p (t d)")[:, 0:T]
        WT = sb("WT", [P, TT, P])
        S = sb("S", [P, P])
        vn = sb("vn", [P, P])
        S0 = sb("S0", [P, NB, P])
        kdm = sb("kdm", [SAMPLE, NB, P])
        WTm = sb("WTm", [P, NB, SAMPLE])
        qdm = sb("qdm", [P, NB, SAMPLE])
        pre = sb("pre", [NB * 3, 3, P])
        tailT = sb("tailT", [P, 3, 27])
        tail = sb("tail", [27, 3, P])
        sc = sb("sc", [P, 6, TT])
        dec = sb("dec", [P, 2 * PT])
        tp = sb("tp", [P, 12])
        gain = sb("gain", [P, 1])
        half = sb("half", [P, 2 * TT])
        ss = sb("ss", [P, 2 * TT])
        co = sb("co", [P, 5, TT])
        ps = ctx.enter_context(nc.psum_tensor("g_ps", [P, 8, 512], F32))

        proj_filled, proj_emptied = sem("proj_filled"), sem("proj_emptied")
        act_filled, act_emptied = sem("act_filled"), sem("act_emptied")
        dve_filled, dve_emptied = sem("dve_filled"), sem("dve_emptied")
        w_loaded, wz_loaded, pre_loaded, S0_loaded, gain_loaded = (
            sem("w_loaded"), sem("wz_loaded"), sem("pre_loaded"), sem("S0_loaded"), sem("gain_loaded"))
        turn_done, o_done = sem("turn_done"), sem("o_done")
        tail_ready, y_half, y_tanh, y_ready, z_tanh = (
            sem("tail_ready"), sem("y_half"), sem("y_tanh"), sem("y_ready"), sem("z_tanh"))
        ug_ready, arg_ready, exp_done = sem("ug_ready"), sem("arg_ready"), sem("exp_done")
        squared, summed, rooted, coef_ready, qk_ready, rk_ready = (
            sem("squared"), sem("summed"), sem("rooted"), sem("coef_ready"), sem("qk_ready"), sem("rk_ready"))
        masked_ready = sem("masked_ready")
        o_ready = sem("o_ready")
        stored = sem("stored")
        a_step, v_step, p_step = sem("a_step"), sem("v_step"), sem("p_step")
        once = sem("once")

        at_end = [("k", 2), ("v", 0)]
        at_start = [("v", 1), ("v", 2), ("z", 0), ("z", 1), ("z", 2)]
        before_all = [("q", 0), ("q", 1), ("q", 2), ("k", 0), ("k", 1)] + at_end

        def act_bank(name, i):
            k = RA.at(name, i)
            return k, ps[:, k.bank, :]

        def dve_bank(name, i):
            k = RD.at(name, i)
            return k, ps[:, k.bank, :]

        def tiles(ap, us):
            return ap[:, us[0]:us[-1] + 1, :]

        def cols(ap, us):
            return ap[:, us[0] * P:(us[-1] + 1) * P]

        def quad(bank, us):
            return bank[:, 0:len(us) * P].rearrange("p (t d) -> p t d", d=P)

        block = ctx.enter_context(nc.Block())

        @block.sync
        def _(sp):
            sp.dma_start(gain[:], gdn_gain.rearrange("a d -> d a")).then_inc(gain_loaded, 16)

            def load_weights(i):
                for n, c0 in enumerate((0, D, 2 * D)):
                    sp.dma_start(W[:, n, :, :], w_rows[:, :, ds(c0 + i * P, P)]).then_inc(w_loaded, 16)

            def load_z_weights(i):
                sp.dma_start(W[:, 3, :, :], w_rows[:, :, ds(C_Z + i * P, P)]).then_inc(wz_loaded, 16)

            def load_rows(i):
                sp.dma_start(pre[:], state_conv[0].rearrange("b r (c n) -> (b r) c n", c=3)[:, :, ds(i * P, P)]
                             ).then_inc(pre_loaded, 16)

            def load_states(i):
                sp.wait_ge(turn_done, i + 1)
                sp.dma_start(S0[:], state_gdn[0].rearrange("b h k v -> h k b v")[ds(i, 1)].rearrange(
                    "a k b v -> (a k) b v")).then_inc(S0_loaded, 16)

            load_weights(0)
            load_rows(0)
            load_z_weights(0)
            with sp.Fori(0, HEADS - 1) as i:
                sp.wait_ge(proj_filled, RP.at("v2", i).full)
                load_weights(i + 1)
                load_states(i)
                sp.wait_ge(dve_filled, RD.at("pre", i).full)
                load_rows(i + 1)
                sp.wait_ge(proj_filled, RP.at("z2", i).full)
                load_z_weights(i + 1)
            load_states(HEADS - 1)

        @block.gpsimd
        def _(gp):
            gp.sem_inc(turn_done, 1)
            gp.memset(half[:], -0.5).then_inc(once, 1)
            gp.memset(X3[:, :, 0:3], 0.0).then_inc(once, 1)
            gp.wait_ge(once, 2)
            with gp.Fori(0, HEADS) as i:
                n = Count(i, 2)

                def step(ins):
                    ins.then_inc(p_step, 1)
                    gp.wait_ge(p_step, n.next())

                gp.wait_ge(summed, 2 * i + 1)
                gp.tensor_tensor(ss[:], ss[:], half[:], ALU.pow).then_inc(rooted, 1)
                gp.wait_ge(rooted, 2 * i + 1)
                gp.wait_ge(coef_ready, i + 1)
                gp.wait_ge(act_emptied, RA.at("tv2", i).done)
                step(gp.tensor_tensor(Rk, tok[:, 1, :, :], rep(co[:, 4, :], 2, P), ALU.mult))
                step(gp.tensor_tensor(tok[:, 2, :, :], tok[:, 2, :, :], rep(sc[:, 1, :], 2, P), ALU.mult))
                gp.wait_ge(qk_ready, i + 1)
                gp.tensor_tensor(tok[:, 1, :, :], tok[:, 1, :, :], rep(co[:, 3, :], 2, P), ALU.mult
                                 ).then_inc(rk_ready, 1)
                gp.wait_ge(rk_ready, i + 1)
                gp.wait_ge(dve_emptied, RD.at("tail", i).done)
                gp.dma_start(conv_p[0, 0].rearrange("r (c n) -> r c n", c=3)[:, :, ds(i * P, P)], tail[0:3, :, :]
                             ).then_inc(stored, 16)
                gp.dma_start(conv_s[0].rearrange("b r (c n) -> (b r) c n", c=3)[:, :, ds(i * P, P)], tail[3:27, :, :]
                             ).then_inc(stored, 16)
                gp.wait_ge(dve_emptied, RD.at("S8b", i).done)
                gp.dma_start(gdn_p[0, 0, ds(i, 1)].rearrange("a k v -> (a k) v"), S[:]).then_inc(stored, 16)
                gp.dma_start(gdn_s[0].rearrange("b h k v -> h k b v")[ds(i, 1)].rearrange("a k b v -> (a k) b v"),
                             S0[:]).then_inc(stored, 16)
                gp.wait_ge(summed, 2 * i + 2)
                gp.tensor_tensor(ss[:, 0:TT], ss[:, 0:TT], half[:, 0:TT], ALU.pow).then_inc(rooted, 1)
                gp.wait_ge(rooted, 2 * i + 2)
                gp.wait_ge(stored, 64 * i + 64)
                gp.wait_ge(o_done, i + 1)
                gp.sem_inc(turn_done, 1)
                n.end()

        @block.scalar
        def _(act):
            def evac(head, x, s):
                (t0, w), c_ = THIRDS[s], "qkvz".index(x)
                k = RP.at(f"{x}{s}", head)
                bank = ps[:, k.bank, :]
                act.wait_ge(proj_filled, k.full)
                if x == "z":
                    ins = act.activation(zh[:, t0:t0 + w], bank[:, 0:w], ACT.Copy, scale=0.5)
                else:
                    prompt = min(w, SEQ - t0)
                    ins = act.copy(X3[:, c_, 3 + t0:3 + t0 + prompt], bank[:, 0:prompt])
                    if prompt < w:
                        ins = act.copy(X3[:, c_, 3 + SEQ:XW].rearrange("p (b s) -> p b s", s=7)[:, :, 3:7],
                                       bank[:, prompt:w].rearrange("p (b s) -> p b s", s=NS))
                ins.then_inc(proj_emptied, 1)

            def head_turn(i, more):
                n = Count(i, 1)
                act.wait_ge(turn_done, i + 1)
                for x, s in at_start:
                    evac(i, x, s)
                act.wait_ge(proj_emptied, RP.at("z2", i).done)
                act.activation(zt[:], zh[:], ACT.Tanh).then_inc(z_tanh, 1)
                for c_ in range(3):
                    act.wait_ge(y_half, 3 * i + c_ + 1)
                    act.activation(T3[:, c_, :], Y3[:, c_, 0:T], ACT.Tanh).then_inc(y_tanh, 1)
                for c_, x in enumerate("qkv"):
                    for u, us in enumerate(tiles_of):
                        k, bank = act_bank(f"t{x}{u}", i)
                        act.wait_ge(act_filled, k.full)
                        act.copy(tiles(tok[:, c_], us), quad(bank, us)).then_inc(act_emptied, 1)
                    if x == "k":
                        act.wait_ge(act_emptied, RA.at("tk2", i).done)
                        act.activation(sq[:], tok[:, 0:2], ACT.Square).then_inc(squared, 1)
                act.wait_ge(arg_ready, i + 1)
                act.wait_ge(summed, 2 * i + 1)
                n_ = act.activation(Elo, Dm[:], ACT.Exp, scale=-1.0)
                n_.then_inc(a_step, 1)
                act.wait_ge(a_step, n.next())
                act.activation(Eup, Ot[:], ACT.Exp).then_inc(exp_done, 1)
                if more:
                    for s in range(3):
                        evac(i + 1, "q", s)
                for x, dst in zip("qdk", (qnT, qdT, knT)):
                    for u, us in enumerate(tiles_of):
                        k, bank = act_bank(f"b{x}{u}", i)
                        act.wait_ge(act_filled, k.full)
                        act.copy(cols(dst, us), bank[:, 0:len(us) * P]).then_inc(act_emptied, 1)
                for m in range(1, len(LEVELS)):
                    for u, us in enumerate(tiles_of):
                        if u == 2 and LEVELS[m] >= NS:
                            continue
                        k, bank = act_bank(f"T{m}{u}", i)
                        act.wait_ge(act_filled, k.full)
                        act.copy(tiles(Tm, us), quad(bank, us)).then_inc(act_emptied, 1)
                for u, us in enumerate(tiles_of):
                    k, bank = act_bank(f"W{u}", i)
                    act.wait_ge(act_filled, k.full)
                    act.activation(tiles(WT, us), quad(bank, us), ACT.Copy, scale=-1.0).then_inc(act_emptied, 1)
                for t in range(TT):
                    k, bank = act_bank(f"O{t}", i)
                    r = P if t < PT else SAMPLE
                    act.wait_ge(act_filled, k.full)
                    act.copy(Ot[0:r, t, :], bank[0:r, 0:P]).then_inc(act_emptied, 1)
                    if more and t in (3, 7):
                        evac(i + 1, "k", t // 4)
                act.wait_ge(act_emptied, RA.at("O8", i).done)
                act.activation(Dm[:], Ot[:], ACT.Square).then_inc(squared, 1)
                if more:
                    for x, s in at_end:
                        evac(i + 1, x, s)
                n.end()

            for x, s in before_all:
                evac(0, x, s)
            with act.Fori(0, HEADS - 1) as i:
                head_turn(i, True)
            head_turn(HEADS - 1, False)

        @block.tensor
        def _(pe):
            def project(head, x, s, k0=0, k1=KT):
                (t0, w), c_ = THIRDS[s], "qkvz".index(x)
                k = RP.at(f"{x}{s}", head)
                if k0 == 0:
                    pe.wait_ge(proj_emptied, k.free)
                    if s == 0 and x in "qz":
                        if x == "z":
                            pe.wait_ge(wz_loaded, 16 * head + 16)
                        else:
                            pe.wait_ge(w_loaded, 48 * head + 48)
                for kt in range(k0, k1):
                    ins = pe.matmul(ps[:, k.bank, 0:w], W[:, c_, kt, :], hT[:, kt, t0:t0 + w],
                                    start=kt == 0, stop=kt == KT - 1)
                if k1 == KT:
                    ins.then_inc(proj_filled, 1)

            def made_by(m):
                return ("A", "Y0")[m] if m < 2 else f"U{m - 1}"

            def head_turn(i, more):
                k, bank = dve_bank("pre", i)
                pe.wait_ge(dve_emptied, k.free)
                pe.wait_ge(pre_loaded, 16 * i + 16)
                for c_ in range(3):
                    ins = pe.matmul(bank[:, c_ * 24:c_ * 24 + 24], pre[:, c_, :], c["ident"][0:24, 0:24],
                                    start=True, stop=True)
                ins.then_inc(dve_filled, 1)
                for x, s in at_start:
                    project(i, x, s)
                k, bank = dve_bank("tail", i)
                pe.wait_ge(dve_emptied, k.free)
                pe.wait_ge(tail_ready, i + 1)
                for c_ in range(3):
                    ins = pe.transpose(bank[0:27, c_ * P:(c_ + 1) * P], tailT[:, c_, :], c["ident"])
                ins.then_inc(dve_filled, 1)
                pe.wait_ge(ug_ready, i + 1)
                for u, us in enumerate(tiles_of):
                    k, bank = dve_bank(f"G{u}", i)
                    pe.wait_ge(dve_emptied, k.free)
                    pe.matmul(bank[:, 0:len(us) * P], c["ones"], tiles(UG, us).rearrange("p t d -> p (t d)"),
                              start=True, stop=True).then_inc(dve_filled, 1)
                for c_, x in enumerate("qkv"):
                    pe.wait_ge(y_ready, 3 * i + c_ + 1)
                    for u, us in enumerate(tiles_of):
                        k, bank = act_bank(f"t{x}{u}", i)
                        pe.wait_ge(act_emptied, k.free)
                        for q, t in enumerate(us):
                            ins = pe.transpose(bank[:, q * P:(q + 1) * P], Y3[:, c_, t * P:(t + 1) * P], c["ident"])
                        ins.then_inc(act_filled, 1)
                if more:
                    for s in range(3):
                        project(i + 1, "q", s)
                pe.wait_ge(qk_ready, i + 1)
                for x, src in zip("qdk", (qn, tok[:, 0], kn)):
                    for u, us in enumerate(tiles_of):
                        k, bank = act_bank(f"b{x}{u}", i)
                        pe.wait_ge(act_emptied, k.free)
                        for q, t in enumerate(us):
                            ins = pe.transpose(bank[:, q * P:(q + 1) * P], src[:, t, :], c["ident"])
                        ins.then_inc(act_filled, 1)
                pe.wait_ge(act_emptied, RA.at("bk2", i).done)
                for x, rhs in (("A", knT), ("Q", qnT)):
                    for u, us in enumerate(tiles_of):
                        k, bank = dve_bank(f"{x}{u}", i)
                        pe.wait_ge(dve_emptied, k.free)
                        for q, t in enumerate(us):
                            ins = pe.matmul(bank[:, q * P:(q + 1) * P], knT[:, t * P:(t + 1) * P],
                                            rhs[:, t * P:(t + 1) * P], start=True, stop=True)
                        ins.then_inc(dve_filled, 1)
                for m in range(len(LEVELS)):
                    groups = [(u, us) for u, us in enumerate(tiles_of) if u < 2 or LEVELS[m] < NS]
                    for u, us in groups:
                        k, bank = dve_bank(f"Y{m}{u}", i)
                        pe.wait_ge(dve_emptied, k.free)
                        pe.wait_ge(dve_emptied, RD.at(f"{made_by(m)}{u}", i).done)
                        for q, t in enumerate(us):
                            if m == 0:
                                ins = pe.transpose(bank[:, q * P:(q + 1) * P], Elo[:, t, :], c["ident"])
                            else:
                                ins = pe.matmul(bank[:, q * P:(q + 1) * P], Elo[:, t, :], TTm[:, t, :],
                                                start=True, stop=True)
                        ins.then_inc(dve_filled, 1)
                    if m == 0:
                        continue
                    for u, us in groups:
                        k, bank = act_bank(f"T{m}{u}", i)
                        pe.wait_ge(act_emptied, k.free)
                        for q, t in enumerate(us):
                            ins = pe.transpose(bank[:, q * P:(q + 1) * P], TTm[:, t, :], c["ident"])
                        ins.then_inc(act_filled, 1)
                    for u, us in groups:
                        k, bank = dve_bank(f"U{m}{u}", i)
                        pe.wait_ge(dve_emptied, k.free)
                        pe.wait_ge(dve_emptied, RD.at(f"Y{m}{u}", i).done)
                        pe.wait_ge(act_emptied, RA.at(f"T{m}{u}", i).done)
                        for q, t in enumerate(us):
                            ins = pe.matmul(bank[:, q * P:(q + 1) * P], Tm[:, t, :], YT[:, t, :], start=True, stop=True)
                        ins.then_inc(dve_filled, 1)
                pe.wait_ge(rk_ready, i + 1)
                for u, us in enumerate(tiles_of):
                    k, bank = act_bank(f"W{u}", i)
                    pe.wait_ge(act_emptied, k.free)
                    pe.wait_ge(dve_emptied, RD.at(f"U{len(LEVELS) - 1 if u < 2 else 1}{u}", i).done)
                    for q, t in enumerate(us):
                        ins = pe.matmul(bank[:, q * P:(q + 1) * P], Rk[:, t, :], TTm[:, t, :], start=True, stop=True)
                    ins.then_inc(act_filled, 1)
                pe.wait_ge(act_emptied, RA.at("W2", i).done)
                for t in range(PT):
                    k, bank = dve_bank(f"V{t}", i)
                    pe.wait_ge(dve_emptied, k.free)
                    pe.matmul(bank[:, 0:P], TTm[:, t, :], tok[:, 2, t, :], start=True, stop=False)
                    if more:
                        project(i + 1, "k", t // 4, 2 * t % KT, 2 * t % KT + 1)
                    if t:
                        pe.wait_ge(dve_emptied, RD.at(f"S{t - 1}", i).done)
                    pe.matmul(bank[:, 0:P], WT[:, t, :], S[:], start=False, stop=True).then_inc(dve_filled, 1)
                    k, obank = act_bank(f"O{t}", i)
                    pe.wait_ge(act_emptied, k.free)
                    pe.matmul(obank[:, 0:P], qdT[:, t * P:(t + 1) * P], S[:], start=True, stop=False)
                    if more:
                        project(i + 1, "k", t // 4, 2 * t % KT + 1, 2 * t % KT + 2)
                    pe.wait_ge(dve_emptied, RD.at(f"V{t}", i).done)
                    pe.matmul(obank[:, 0:P], Eup[:, t, :], vn[:], start=False, stop=True).then_inc(act_filled, 1)
                    k, bank = dve_bank(f"S{t}", i)
                    pe.wait_ge(dve_emptied, k.free)
                    pe.matmul(bank[:, 0:P], tok[:, 1, t, :], vn[:], start=True, stop=True).then_inc(dve_filled, 1)
                k, bank = dve_bank("V8", i)
                pe.wait_ge(dve_emptied, k.free)
                pe.wait_ge(masked_ready, i + 1)
                pe.wait_ge(S0_loaded, 16 * i + 16)
                pe.matmul(bank[0:SAMPLE, 0:P], TTm[:, PT, 0:SAMPLE], tok[:, 2, PT, :], start=True, stop=False)
                for b in range(NB):
                    ins = pe.matmul(bank[0:SAMPLE, 0:P], WTm[:, b, :], S0[:, b, :], start=False, stop=b == NB - 1)
                ins.then_inc(dve_filled, 1)
                k, obank = act_bank("O8", i)
                pe.wait_ge(act_emptied, k.free)
                for b in range(NB):
                    pe.matmul(obank[0:SAMPLE, 0:P], qdm[:, b, :], S0[:, b, :], start=b == 0, stop=False)
                pe.wait_ge(dve_emptied, RD.at("V8", i).done)
                pe.matmul(obank[0:SAMPLE, 0:P], Eup[:, PT, 0:SAMPLE], vn[:],
                          start=False, stop=True).then_inc(act_filled, 1)
                for x in range(2):
                    k, bank = dve_bank(f"S8{'ab'[x]}", i)
                    pe.wait_ge(dve_emptied, k.free)
                    for q in range(4):
                        ins = pe.matmul(bank[:, q * P:(q + 1) * P], kdm[:, 4 * x + q, :], vn[0:SAMPLE, :],
                                        start=True, stop=True)
                    ins.then_inc(dve_filled, 1)
                if more:
                    for x, s in at_end:
                        project(i + 1, x, s)
                pe.wait_ge(o_ready, i + 1)
                for u, us in enumerate(tiles_of):
                    k, bank = dve_bank(f"N{u}", i)
                    pe.wait_ge(dve_emptied, k.free)
                    for q, t in enumerate(us):
                        ins = pe.transpose(bank[:, q * P:(q + 1) * P], Ot[:, t, :], c["ident"])
                    ins.then_inc(dve_filled, 1)

            for x, s in before_all:
                project(0, x, s)
            with pe.Fori(0, HEADS - 1) as i:
                head_turn(i, True)
            head_turn(HEADS - 1, False)

        @block.vector
        def _(v):
            v.sem_inc(proj_emptied, 2)
            v.sem_inc(act_emptied, 3)
            v.sem_inc(dve_emptied, 3)
            v.wait_ge(gain_loaded, 16)
            v.wait_ge(once, 2)

            with v.Fori(0, HEADS) as i:
                n = Count(i, 56)

                def step(ins):
                    ins.then_inc(v_step, 1)
                    v.wait_ge(v_step, n.next())

                v.wait_ge(turn_done, i + 1)
                one = ds(i, 1)
                step(v.tensor_copy(sc[:], g.SC[:, one].rearrange("p a k t -> p (a k) t")))
                step(v.tensor_copy(dec[:], g.DEC[:, one].rearrange("p a t -> p (a t)")))
                step(v.tensor_copy(tp[:], g.taps[:, one].rearrange("p a c j -> p (a c j)")))
                step(v.memset(S[:], 0.0))
                step(v.memset(Y3[:, :, T:TP], 0.0))
                step(v.tensor_tensor(UG[:, 0:PT, :], rep(c["cum"][:, 0, :], 1, PT), rep(sc[:, 5, 0:PT], 2, P), ALU.mult))
                v.tensor_scalar(UG[:, PT, :], c["cum"][:, 1, :], sc[:, 5, PT:TT], None, ALU.mult).then_inc(ug_ready, 1)
                k, bank = dve_bank("pre", i)
                v.wait_ge(dve_filled, k.full)
                for c_ in range(3):
                    ins = v.tensor_copy(X3[:, c_, 3 + SEQ:XW].rearrange("p (b s) -> p b s", s=7)[:, :, 0:3],
                                        bank[:, c_ * 24:c_ * 24 + 24].rearrange("p (b s) -> p b s", s=3))
                    if c_ < 2:
                        step(ins)
                ins.then_inc(dve_emptied, 1)
                v.wait_ge(dve_emptied, k.done)
                for c_, x in enumerate("qkv"):
                    v.wait_ge(proj_emptied, RP.at(f"{x}2", i).done)
                    seqs = X3[:, c_, 3 + SEQ:XW].rearrange("p (b s) -> p b s", s=7)
                    yp = Y3[:, c_, 0:SEQ]
                    ys = Y3[:, c_, SEQ:T].rearrange("p (b s) -> p b s", s=NS)
                    for j in range(CONV):
                        tap = tp[:, c_ * CONV + j:c_ * CONV + j + 1]
                        for y, src in ((yp, X3[:, c_, j:j + SEQ]), (ys, seqs[:, :, j:j + NS])):
                            if j == 0:
                                ins = v.tensor_scalar(y, src, tap, None, ALU.mult)
                            else:
                                ins = v.scalar_tensor_tensor(y, src, tap, y, ALU.mult, ALU.add)
                            if j < CONV - 1 or y is yp:
                                step(ins)
                    ins.then_inc(y_half, 1)
                v.wait_ge(y_half, 3 * i + 3)
                step(v.tensor_copy(tailT[:, :, 0:3], X3[:, :, SEQ:SEQ + 3]))
                for c_ in range(3):
                    ins = v.tensor_copy(tailT[:, c_, 3:27].rearrange("p (b s) -> p b s", s=3),
                                        X3[:, c_, 3 + SEQ:XW].rearrange("p (b s) -> p b s", s=7)[:, :, 4:7])
                    if c_ < 2:
                        step(ins)
                ins.then_inc(tail_ready, 1)
                v.wait_ge(tail_ready, i + 1)
                v.wait_ge(z_tanh, i + 1)
                step(v.scalar_tensor_tensor(zh[:], zt[:], 1.0, zh[:], ALU.add, ALU.mult))
                for c_ in range(3):
                    v.wait_ge(y_tanh, 3 * i + c_ + 1)
                    v.scalar_tensor_tensor(Y3[:, c_, 0:T], T3[:, c_, :], 1.0, Y3[:, c_, 0:T], ALU.add, ALU.mult
                                           ).then_inc(y_ready, 1)
                v.wait_ge(y_ready, 3 * i + 3)
                k, bank = dve_bank("tail", i)
                v.wait_ge(dve_filled, k.full)
                v.tensor_copy(tail[:].rearrange("p c d -> p (c d)"), bank[0:27, 0:3 * P]).then_inc(dve_emptied, 1)
                for u, us in enumerate(tiles_of):
                    k, bank = dve_bank(f"G{u}", i)
                    v.wait_ge(dve_filled, k.full)
                    v.tensor_tensor(tiles(Dm, us), quad(bank, us), rep(sc[:, 0, us[0]:us[-1] + 1], 2, P), ALU.subtract
                                    ).then_inc(dve_emptied, 1)
                v.wait_ge(dve_emptied, RD.at("G2", i).done)
                step(v.tensor_tensor(Ot[:, 0:PT, :], Dm[:, 0:PT, :], rep(c["upper"][:, 0, :], 1, PT), ALU.add))
                step(v.tensor_tensor(Ot[:, PT, :], Dm[:, PT, :], c["upper"][:, 1, :], ALU.add))
                step(v.tensor_tensor(Dm[:, 0:PT, :], Dm[:, 0:PT, :], rep(c["lower"][:, 0, :], 1, PT), ALU.add))
                v.tensor_tensor(Dm[:, PT, :], Dm[:, PT, :], c["lower"][:, 1, :], ALU.add).then_inc(arg_ready, 1)
                v.wait_ge(arg_ready, i + 1)
                v.wait_ge(squared, 2 * i + 1)
                step(v.tensor_reduce(ss[:].rearrange("p (c t) -> p c t", c=2), sq[:], AX, ALU.add))
                v.tensor_scalar(ss[:], ss[:], EPS, None, ALU.add).then_inc(summed, 1)
                v.wait_ge(rooted, 2 * i + 1)
                step(v.tensor_scalar(co[:, 0, :], ss[:, 0:TT], DH ** -0.5, None, ALU.mult))
                step(v.tensor_tensor(co[:, 1, :], co[:, 0, :], sc[:, 2, :], ALU.mult))
                step(v.tensor_copy(co[:, 2, :], ss[:, TT:2 * TT]))
                step(v.tensor_tensor(co[:, 3, :], co[:, 2, :], sc[:, 3, :], ALU.mult))
                v.tensor_tensor(co[:, 4, :], co[:, 2, :], sc[:, 4, :], ALU.mult).then_inc(coef_ready, 1)
                v.wait_ge(act_filled, RA.at("tv2", i).full)
                step(v.tensor_tensor(qn, tok[:, 0, :, :], rep(co[:, 0, :], 2, P), ALU.mult))
                step(v.tensor_tensor(tok[:, 0, :, :], tok[:, 0, :, :], rep(co[:, 1, :], 2, P), ALU.mult))
                v.tensor_tensor(kn, tok[:, 1, :, :], rep(co[:, 2, :], 2, P), ALU.mult).then_inc(qk_ready, 1)
                v.wait_ge(exp_done, i + 1)
                for u, us in enumerate(tiles_of):
                    k, bank = dve_bank(f"A{u}", i)
                    v.wait_ge(dve_filled, k.full)
                    for q, t in enumerate(us):
                        ins = v.scalar_tensor_tensor(Elo[:, t, :], bank[:, q * P:(q + 1) * P], sc[:, 1, t:t + 1],
                                                     Elo[:, t, :], ALU.mult, ALU.mult)
                    ins.then_inc(dve_emptied, 1)
                for u, us in enumerate(tiles_of):
                    k, bank = dve_bank(f"Q{u}", i)
                    v.wait_ge(dve_filled, k.full)
                    v.tensor_tensor(tiles(Eup, us), quad(bank, us), tiles(Eup, us), ALU.mult).then_inc(dve_emptied, 1)
                for m in range(len(LEVELS)):
                    groups = [(u, us) for u, us in enumerate(tiles_of) if u < 2 or LEVELS[m] < NS]
                    for u, us in groups:
                        k, bank = dve_bank(f"Y{m}{u}", i)
                        v.wait_ge(dve_filled, k.full)
                        mask = rep(c["level"][:, m, :], 1, len(us))
                        if m == 0:
                            step(v.tensor_tensor(tiles(TTm, us), quad(bank, us), mask, ALU.mult))
                            v.tensor_tensor(tiles(TTm, us), tiles(TTm, us), rep(c["ident"], 1, len(us)), ALU.add
                                            ).then_inc(dve_emptied, 1)
                        else:
                            v.tensor_tensor(tiles(YT, us), quad(bank, us), mask, ALU.mult).then_inc(dve_emptied, 1)
                    for u, us in groups if m else ():
                        k, bank = dve_bank(f"U{m}{u}", i)
                        v.wait_ge(dve_filled, k.full)
                        v.tensor_tensor(tiles(TTm, us), quad(bank, us), tiles(TTm, us), ALU.add
                                        ).then_inc(dve_emptied, 1)
                for t in range(PT):
                    k, bank = dve_bank(f"V{t}", i)
                    v.wait_ge(dve_filled, k.full)
                    v.tensor_copy(vn[:], bank[:, 0:P]).then_inc(dve_emptied, 1)
                    k, bank = dve_bank(f"S{t}", i)
                    v.wait_ge(dve_filled, k.full)
                    v.scalar_tensor_tensor(S[:], S[:], dec[:, t:t + 1], bank[:, 0:P], ALU.mult, ALU.add
                                           ).then_inc(dve_emptied, 1)
                    if t == 0:
                        v.wait_ge(act_emptied, RA.at("W2", i).done)
                        v.wait_ge(rk_ready, i + 1)
                        step(v.memset(Ot[:, PT, :], 0.0))
                        step(v.tensor_tensor(WTm[:], rep(WT[:, PT, 0:SAMPLE], 1, NB), c["seqcol"], ALU.mult))
                        step(v.tensor_tensor(qdm[:], rep(qdT[:, SEQ:T], 1, NB), c["seqcol"], ALU.mult))
                        v.tensor_tensor(kdm[:], rep(tok[0:SAMPLE, 1, PT, :], 1, NB), rep(c["seqrow"][0:SAMPLE, :], 2, P),
                                        ALU.mult).then_inc(masked_ready, 1)
                k, bank = dve_bank("V8", i)
                v.wait_ge(dve_filled, k.full)
                v.tensor_copy(vn[0:SAMPLE, :], bank[0:SAMPLE, 0:P]).then_inc(dve_emptied, 1)
                for x in range(2):
                    k, bank = dve_bank(f"S8{'ab'[x]}", i)
                    v.wait_ge(dve_filled, k.full)
                    for q in range(4):
                        b = 4 * x + q
                        ins = v.scalar_tensor_tensor(S0[:, b, :], S0[:, b, :], dec[:, PT + b:PT + b + 1],
                                                     bank[:, q * P:(q + 1) * P], ALU.mult, ALU.add)
                        if q < 3:
                            step(ins)
                    ins.then_inc(dve_emptied, 1)
                v.wait_ge(squared, 2 * i + 2)
                step(v.tensor_reduce(ss[:, 0:TT], Dm[:], AX, ALU.add))
                v.tensor_scalar(ss[:, 0:TT], ss[:, 0:TT], 1.0 / DH, EPS, ALU.mult, ALU.add).then_inc(summed, 1)
                v.wait_ge(rooted, 2 * i + 2)
                v.tensor_tensor(Ot[:], Ot[:], rep(ss[:, 0:TT], 2, P), ALU.mult).then_inc(o_ready, 1)
                for u, us in enumerate(tiles_of):
                    k, bank = dve_bank(f"N{u}", i)
                    v.wait_ge(dve_filled, k.full)
                    w = len(us) * P if u < 2 else SAMPLE
                    t0 = us[0] * P
                    v.scalar_tensor_tensor(oAT[:, ds(i, 1), t0:t0 + w].rearrange("p a n -> p (a n)"), bank[:, 0:w],
                                           gain[:, 0:1], zh[:, t0:t0 + w], ALU.mult, ALU.mult
                                           ).then_inc(dve_emptied, 1)
                v.wait_ge(dve_emptied, RD.at("N2", i).done)
                v.sem_inc(o_done, 1)
                n.end()


def load_pair(nc, sp, W, w_in, r, loaded):
    w_rows = w_in[0].rearrange("(k p) n -> p k n", p=P)
    for n, c0 in enumerate((C_Q, C_ZB)):
        for gr in range(2):
            sp.dma_start(W[:, n, :, gr * DN:(gr + 1) * DN], w_rows[:, :, ds(c0 + gr * 256 + r * DN, DN)]
                         ).then_inc(loaded, 16)


def stage_kv(nc, g, w_in, pos, lin, state_win, kv_p, kv_s, win_s):
    KV, hT, posT, blk = g.KV, g.hT, g.posT, g.blk
    with ExitStack() as ctx:
        def sb(name, shape, dt=F32):
            return ctx.enter_context(nc.sbuf_tensor("k_" + name, shape, dt))

        def sem(name):
            return ctx.enter_context(nc.semaphore("k_" + name))

        W = sb("W", [P, KT, 6 * P])
        cmpT = sb("cmpT", [P, 2, SEQ])
        pos_rows = sb("pos_rows", [CL, 2, P])
        CW = sb("CW", [P, 2, CL, P])
        vcT = sb("vcT", [P, NCB])
        ps = ctx.enter_context(nc.psum_tensor("k_ps", [P, 8, 512], F32))
        w_loaded = [sem(f"w_loaded{s}") for s in range(2)]
        pos_loaded, lin_loaded, blk_clear = sem("pos_loaded"), sem("lin_loaded"), sem("blk_clear")
        act_filled, act_emptied = sem("act_filled"), sem("act_emptied")
        dve_filled, dve_emptied = sem("dve_filled"), sem("dve_emptied")
        cw_ready, stored, stores, pair_loaded = sem("cw_ready"), sem("stored"), sem("stores"), sem("pair_loaded")
        turns = [(n, u) for n in range(4) for u in range(2 if n < 2 else 3)]
        RA = Ring([0, 1, 2, 3], [f"a{t}" for t in range(TT)] + [f"t{n}{u}" for n, u in turns if u != 1] + ["kc"])
        RD = Ring([4, 5, 6, 7], ["pos"] + [f"b{t}" for t in range(TT)] + [f"t{n}{u}" for n, u in turns if u == 1]
                  + ["vcT", "vc"])
        dst = [cmpT[:, 0, :], cmpT[:, 1, :], g.slcT, g.winT]
        block = ctx.enter_context(nc.Block())

        def turned(n, u):
            k = (RD if u == 1 else RA).at(f"t{n}{u}")
            w = 4 * P if u < 2 else SAMPLE
            return k, dst[n][:, u * 512:u * 512 + w], ps[:, k.bank, 0:w]

        @block.sync
        def _(sp):
            for s in range(2):
                sp.dma_start(W[:, :, s * 384:(s + 1) * 384],
                             w_in[0].rearrange("(k p) n -> p k n", p=P)[:, :, C_KV + s * 384:C_KV + (s + 1) * 384]
                             ).then_inc(w_loaded[s], 16)
            for n in range(2):
                for half in range(2):
                    sp.dma_start(pos_rows[:, n, half * DN:(half + 1) * DN], pos[n][0]).then_inc(pos_loaded, 16)
            sp.wait_ge(blk_clear, 1)
            for n in range(2):
                for half in range(2):
                    r = slice(half * DN, (half + 1) * DN)
                    sp.dma_start(blk[r, n, r], lin[n][0]).then_inc(lin_loaded, 16)
            load_pair(nc, sp, g.Wpair, w_in, 0, pair_loaded)
            for n in range(2):
                sp.dma_start(win_s[n][0].rearrange("b w g d -> b w (g d)")[:, 0:WIN - NS, :],
                             state_win[n][0].rearrange("b w g d -> b w (g d)")[:, NS:WIN, :]).then_inc(stores, 16)
            sp.wait_ge(act_emptied, RA.at(f"a{PT}").done)
            sp.wait_ge(dve_emptied, RD.at(f"b{PT}").done)
            for n in range(6):
                part = slice(n * P, (n + 1) * P)
                src, t0 = (KV[:, 0:PT, part], 0) if n < 4 else (KV[:, 4:PT, part], 4)
                sp.dma_start(kv_p[n][0, 0].rearrange("(t p) g d -> p t (g d)", p=P), src).then_inc(stores, 16)
                rows = KV[0:SAMPLE, PT, part]
                if n < 4:
                    sp.dma_start(kv_s[n][0].rearrange("b s g d -> (b s) (g d)"), rows).then_inc(stores, 16)
                else:
                    for b in range(NB):
                        sp.dma_start(win_s[n - 4][0, b].rearrange("w g d -> w (g d)")[WIN - NS:WIN, :],
                                     KV[b * NS:(b + 1) * NS, PT, part]).then_inc(stores, 16)
            sp.wait_ge(pair_loaded, 64)
            sp.wait_ge(stores, 16 * (6 + 4 + 2 * NB + 2))

        @block.gpsimd
        def _(gp):
            gp.memset(blk[:], 0.0).then_inc(blk_clear, 1)

        @block.tensor
        def _(pe):
            k = RD.at("pos")
            pe.wait_ge(dve_emptied, k.free)
            pe.wait_ge(pos_loaded, 64)
            for n in range(2):
                ins = pe.transpose(ps[:, k.bank, n * CL:(n + 1) * CL], pos_rows[:, n, :], g.ident[0:CL, 0:CL])
            ins.then_inc(dve_filled, 1)
            for t in range(TT):
                n = P if t < PT else SAMPLE
                for s, (R, emptied, filled) in enumerate(((RA, act_emptied, act_filled), (RD, dve_emptied, dve_filled))):
                    k = R.at(f"{'ab'[s]}{t}")
                    pe.wait_ge(emptied, k.free)
                    if t == 0:
                        pe.wait_ge(w_loaded[s], 16)
                    for kt in range(KT):
                        ins = pe.matmul(ps[0:n, k.bank, 0:384], hT[:, kt, t * P:t * P + n],
                                        W[:, kt, s * 384:(s + 1) * 384], start=kt == 0, stop=kt == KT - 1)
                    ins.then_inc(filled, 1)
            pe.wait_ge(act_emptied, RA.at(f"a{PT}").done)
            pe.wait_ge(dve_emptied, RD.at(f"b{PT}").done)
            for n, u in turns:
                k, _, bank = turned(n, u)
                pe.wait_ge(dve_emptied if u == 1 else act_emptied, k.free)
                part = (0, 1, 2, 4)[n] * P
                for q, t in enumerate(range(4 * u, min(4 * u + 4, TT))):
                    r = P if t < PT else SAMPLE
                    ins = pe.transpose(bank[:, q * P:q * P + r], KV[0:r, t, part:part + P], g.ident[0:r, 0:r])
                ins.then_inc(dve_filled if u == 1 else act_filled, 1)
            pe.wait_ge(cw_ready, 2)
            for n, (R, name, emptied, filled) in enumerate(((RA, "kc", act_emptied, act_filled),
                                                            (RD, "vcT", dve_emptied, dve_filled))):
                k = R.at(name)
                pe.wait_ge(emptied, k.free)
                pe.wait_ge(act_emptied, RA.at(f"t{n}0").done)
                pe.wait_ge(dve_emptied, RD.at(f"t{n}1").done)
                for j in range(CL):
                    ins = pe.matmul(ps[:, k.bank, 0:NCB], CW[:, n, j, :], cmpT[:, n, j:j + CS * (NCB - 1) + 1:CS],
                                    start=j == 0, stop=j == CL - 1)
                ins.then_inc(filled, 1)
            k = RD.at("vc")
            pe.wait_ge(dve_emptied, RD.at("vcT").done)
            pe.transpose(ps[0:NCB, k.bank, 0:P], vcT[:], g.ident).then_inc(dve_filled, 1)

        @block.scalar
        def _(act):
            for t in range(TT):
                n = P if t < PT else SAMPLE
                k = RA.at(f"a{t}")
                act.wait_ge(act_filled, k.full)
                act.copy(KV[0:n, t, 0:384], ps[0:n, k.bank, 0:384]).then_inc(act_emptied, 1)
            for n, u in turns:
                if u != 1:
                    k, to, bank = turned(n, u)
                    act.wait_ge(act_filled, k.full)
                    act.copy(to, bank).then_inc(act_emptied, 1)
            k = RA.at("kc")
            act.wait_ge(act_filled, k.full)
            act.copy(g.kcT[:], ps[:, k.bank, 0:NCB]).then_inc(act_emptied, 1)

        @block.vector
        def _(v):
            v.sem_inc(act_emptied, 4)
            v.sem_inc(dve_emptied, 4)
            k = RD.at("pos")
            v.wait_ge(dve_filled, k.full)
            v.tensor_copy(posT[:].rearrange("p n j -> p (n j)"), ps[:, k.bank, 0:2 * CL]).then_inc(dve_emptied, 1)
            v.wait_ge(dve_emptied, k.done)
            v.wait_ge(lin_loaded, 64)
            for n in range(2):
                v.tensor_tensor(CW[:, n, :, :], rep(blk[:, n, :], 1, CL), rep(posT[:, n, :], 2, P), ALU.mult
                                ).then_inc(cw_ready, 1)
            for t in range(TT):
                n = P if t < PT else SAMPLE
                k = RD.at(f"b{t}")
                v.wait_ge(dve_filled, k.full)
                v.tensor_copy(KV[0:n, t, 384:768], ps[0:n, k.bank, 0:384]).then_inc(dve_emptied, 1)
            v.wait_ge(dve_emptied, RD.at(f"b{PT}").done)
            v.tensor_copy(g.vS[:, 0, :], KV[0:SAMPLE, PT, 3 * P:4 * P]).then_inc(stored, 1)
            v.tensor_copy(g.vS[:, 1, :], KV[0:SAMPLE, PT, 5 * P:6 * P]).then_inc(stored, 1)
            for n, u in turns:
                if u == 1:
                    k, to, bank = turned(n, u)
                    v.wait_ge(dve_filled, k.full)
                    v.tensor_copy(to, bank).then_inc(dve_emptied, 1)
            v.wait_ge(act_emptied, RA.at("t32").done)
            v.tensor_copy(g.slcS[:], g.slcT[:, SEQ:T]).then_inc(stored, 1)
            v.tensor_copy(g.winS[:], g.winT[:, SEQ:T]).then_inc(stored, 1)
            k = RD.at("vcT")
            v.wait_ge(dve_filled, k.full)
            v.tensor_copy(vcT[:], ps[:, k.bank, 0:NCB]).then_inc(dve_emptied, 1)
            k = RD.at("vc")
            v.wait_ge(dve_filled, k.full)
            v.tensor_copy(g.vc[:], ps[0:NCB, k.bank, 0:P]).then_inc(dve_emptied, 1)


def stage_prompt(nc, g, w_in, nsa_consts):
    KV, hT, oBT = g.KV, g.hT, g.oBT
    parts = nsa_parts()
    units = [(qt, gr) for qt in range(PT) for gr in range(2)]
    NU = len(units)

    def tiles_of(qt):
        return ([("slc", t) for t in range(qt + 1)] + [("win", t) for t in range(max(0, qt - 4), qt + 1)]
                + [("cmp", 0)])

    def groups_of(qt):
        ts = tiles_of(qt)
        return [(u, 4 * u, ts[4 * u:4 * u + 4]) for u in range((len(ts) + 3) // 4)]

    RA = Ring([4, 5], [f"{x}{s}" for x in "qz" for s in range(3)]
              + [f"T{n}{u}" for n, (qt, gr) in enumerate(units) for u, _, _ in groups_of(qt)])
    RO = Ring([6, 7], [f"O{n}" for n in range(NU)])

    with ExitStack() as ctx:
        def sb(name, shape, dt=F32):
            return ctx.enter_context(nc.sbuf_tensor("p_" + name, shape, dt))

        def sem(name):
            return ctx.enter_context(nc.semaphore("p_" + name))

        ctile = sb("ctile", [P, sum(a.size for a in parts.values()) // P])
        c = Packed(ctile, parts)
        W = g.Wpair
        qT = sb("qT", [P, T])
        zh = sb("zh", [P, T])
        WC, CC = SEQ, SEQ + 5 * P
        Pr = [sb(f"Pr{n}", [P, CC + P]) for n in range(3)]
        zt = Pr[0][:, 0:T]
        PTr = sb("PTr", [P, 3, 4, P])
        nmx = sb("nmx", [P, 2, 3])
        rs = sb("rs", [P, 2, 3])
        co = sb("co", [P, 3])
        gst = sb("gst", [P, PT, 2, 3])
        ps = ctx.enter_context(nc.psum_tensor("p_ps", [P, 8, 512], F32))
        s_slc = ps[:, 0:2, :].rearrange("p a n -> p (a n)")
        s_win = ps[:, 2:4, :].rearrange("p a n -> p (a n)")
        c_loaded, w_loaded, turn_done = sem("c_loaded"), sem("w_loaded"), sem("turn_done")
        a_filled, a_emptied, o_filled, o_emptied = sem("a_filled"), sem("a_emptied"), sem("o_filled"), sem("o_emptied")
        slc_scores, win_scores = sem("slc_scores"), sem("win_scores")
        slc_max, win_max = sem("slc_max"), sem("win_max")
        slc_exp, win_exp, weighted = sem("slc_exp"), sem("win_exp"), sem("weighted")
        z_tanh, v_step = sem("z_tanh"), sem("v_step")
        block = ctx.enter_context(nc.Block())

        def nth(i, n):
            return i * NU + n + 1

        @block.sync
        def _(sp):
            sp.dma_start(ctile[:], nsa_consts).then_inc(c_loaded, 16)

            sp.sem_inc(w_loaded, 64)
            with sp.Fori(0, PAIRS - 1) as r:
                sp.wait_ge(a_filled, RA.at("z2", r).full)
                load_pair(nc, sp, W, w_in, r + 1, w_loaded)

        @block.tensor
        def _(pe):
            def scores_slc(i, n):
                qt, gr = units[n]
                rows = slice(gr * DN, (gr + 1) * DN)
                q = qT[rows, qt * P:(qt + 1) * P]
                pe.wait_ge(slc_exp, nth(i, n))
                for k0 in range(0, (qt + 1) * P, 512):
                    w = min(512, (qt + 1) * P - k0)
                    ins = pe.matmul(s_slc[:, k0:k0 + w], q, g.slcT[rows, k0:k0 + w], start=True, stop=True)
                ins.then_inc(slc_scores, 1)

            def scores_win(i, n):
                qt, gr = units[n]
                rows = slice(gr * DN, (gr + 1) * DN)
                q = qT[rows, qt * P:(qt + 1) * P]
                pe.wait_ge(win_exp, nth(i, n))
                w0 = max(0, qt - 4) * P
                for k0 in range(w0, (qt + 1) * P, 512):
                    w = min(512, (qt + 1) * P - k0)
                    pe.matmul(s_win[:, k0 - w0:k0 - w0 + w], q, g.winT[rows, k0:k0 + w], start=True, stop=True)
                pe.matmul(s_win[:, 640:640 + NCB], q, g.kcT[rows, :], start=True, stop=True).then_inc(win_scores, 1)

            def turn(i, n, u, ts):
                qt = units[n][0]
                k = RA.at(f"T{n}{u}", i)
                pe.wait_ge(a_emptied, k.free)
                if u == 0:
                    pe.wait_ge(weighted, nth(i, n))
                for q, (kind, t) in enumerate(ts):
                    c0 = {"slc": t * P, "win": WC + (t - max(0, qt - 4)) * P, "cmp": CC}[kind]
                    ins = pe.transpose(ps[:, k.bank, q * P:(q + 1) * P], Pr[n % 3][:, c0:c0 + P], g.ident)
                ins.then_inc(a_filled, 1)

            def values(i, n, u, at, ts):
                k = RO.at(f"O{n}", i)
                if u == 0:
                    pe.wait_ge(o_emptied, k.free)
                pe.wait_ge(a_emptied, RA.at(f"T{n}{u}", i).done)
                for q, (kind, t) in enumerate(ts):
                    r = NCB if kind == "cmp" else P
                    v = g.vc[:, :] if kind == "cmp" else KV[:, t, {"slc": 3, "win": 5}[kind] * P:][:, 0:P]
                    ins = pe.matmul(ps[:, k.bank, 0:P], v, PTr[0:r, u % 3, q, :], start=at + q == 0,
                                    stop=kind == "cmp")
                if kind == "cmp":
                    ins.then_inc(o_filled, 1)

            def outputs(i, n):
                gs = groups_of(units[n][0])
                for x, (u, at, ts) in enumerate(gs):
                    values(i, n, u, at, ts)
                    if x + 2 < len(gs):
                        turn(i, n, gs[x + 2][0], gs[x + 2][2])

            with pe.Fori(0, PAIRS) as i:
                pe.wait_ge(w_loaded, 64 * i + 64)
                for n, x in enumerate("qz"):
                    for s, (t0, w) in enumerate(THIRDS):
                        k = RA.at(f"{x}{s}", i)
                        pe.wait_ge(a_emptied, k.free)
                        for kt in range(KT):
                            ins = pe.matmul(ps[:, k.bank, 0:w], W[:, n, kt, :], hT[:, kt, t0:t0 + w],
                                            start=kt == 0, stop=kt == KT - 1)
                        ins.then_inc(a_filled, 1)
                pe.wait_ge(a_emptied, RA.at("q2", i).done)
                for n in range(NU + 2):
                    if n < NU:
                        scores_slc(i, n)
                    if n >= 2:
                        for u, _, ts in groups_of(units[n - 2][0])[:2]:
                            turn(i, n - 2, u, ts)
                    if n < NU:
                        scores_win(i, n)
                    if n >= 2:
                        outputs(i, n - 2)

        @block.scalar
        def _(act):
            act.sem_inc(slc_exp, 1)
            act.sem_inc(win_exp, 1)

            def exp_slc(i, n):
                qt, gr = units[n]
                w, m = (qt + 1) * P, n % 2
                act.wait_ge(slc_max, nth(i, n))
                act.activation(Pr[n % 3][:, 0:w], s_slc[:, 0:w], ACT.Exp, bias=nmx[:, m, 0:1], accum_out=rs[:, m, 0:1]
                               ).then_inc(slc_exp, 1)

            def exp_win(i, n):
                qt, gr = units[n]
                ww, m, out = (min(qt, 4) + 1) * P, n % 2, Pr[n % 3]
                act.wait_ge(win_max, nth(i, n))
                act.activation(out[:, WC:WC + ww], s_win[:, 0:ww], ACT.Exp, bias=nmx[:, m, 1:2], accum_out=rs[:, m, 1:2])
                act.activation(out[:, CC:CC + NCB], s_win[:, 640:640 + NCB], ACT.Exp, bias=nmx[:, m, 2:3]
                               ).then_inc(win_exp, 1)

            def evac(i, n, u, at, ts):
                k = RA.at(f"T{n}{u}", i)
                act.wait_ge(a_filled, k.full)
                act.copy(PTr[:, u % 3, 0:len(ts), :].rearrange("p t q -> p (t q)"), ps[:, k.bank, 0:len(ts) * P]
                         ).then_inc(a_emptied, 1)

            with act.Fori(0, PAIRS) as i:
                for x, to, scale in (("q", qT, DN ** -0.5), ("z", zh, 0.5)):
                    if x == "z":
                        act.wait_ge(turn_done, i + 3)
                    for s, (t0, w) in enumerate(THIRDS):
                        k = RA.at(f"{x}{s}", i)
                        act.wait_ge(a_filled, k.full)
                        act.activation(to[:, t0:t0 + w], ps[:, k.bank, 0:w], ACT.Copy, scale=scale
                                       ).then_inc(a_emptied, 1)
                act.wait_ge(a_emptied, RA.at("z2", i).done)
                act.activation(zt[:], zh[:], ACT.Tanh).then_inc(z_tanh, 1)
                for n in range(NU + 2):
                    gs = groups_of(units[n - 2][0]) if n >= 2 else []
                    for x in gs[:2]:
                        evac(i, n - 2, *x)
                    if n < NU:
                        exp_slc(i, n)
                    for x in gs[2:3]:
                        evac(i, n - 2, *x)
                    if n < NU:
                        exp_win(i, n)
                    for x in gs[3:]:
                        evac(i, n - 2, *x)

        @block.vector
        def _(v):
            v.sem_inc(a_emptied, 2)
            v.sem_inc(o_emptied, 2)
            v.wait_ge(c_loaded, 16)
            for n in range(3):
                v.memset(Pr[n][:, CC:CC + P], 0.0).then_inc(turn_done, 1)

            def maxima(i, n, step):
                qt, gr = units[n]
                m = n % 2
                w, ww = (qt + 1) * P, (min(qt, 4) + 1) * P
                v.wait_ge(slc_scores, nth(i, n))
                step(v.tensor_tensor(s_slc[:, w - P:w], s_slc[:, w - P:w], c["causal"], ALU.add))
                v.tensor_reduce(nmx[:, m, 0:1], s_slc[:, 0:w], AX, ALU.max, negate=True).then_inc(slc_max, 1)
                v.wait_ge(win_scores, nth(i, n))
                v.tensor_tensor(s_win[:, ww - P:ww], s_win[:, ww - P:ww], c["causal"], ALU.add).then_inc(v_step, 1)
                if qt >= 4:
                    v.tensor_tensor(s_win[:, 0:P], s_win[:, 0:P], c["edge"], ALU.add).then_inc(v_step, 1)
                    cnt.next()
                cnt.next()
                step(v.tensor_tensor(s_win[:, 640:640 + NCB], s_win[:, 640:640 + NCB], c["unseen"][:, qt, :], ALU.add))
                v.tensor_reduce(nmx[:, m, 1:2], s_win[:, 0:ww], AX, ALU.max, negate=True).then_inc(v_step, 1)
                cnt.next()
                v.tensor_reduce(nmx[:, m, 2:3], s_win[:, 640:640 + NCB], AX, ALU.max, negate=True).then_inc(v_step, 1)
                v.wait_ge(v_step, cnt.next())
                v.sem_inc(win_max, 1)

            def weigh(i, n, step):
                qt, gr = units[n]
                m, pr = n % 2, Pr[n % 3]
                w, ww = (qt + 1) * P, (min(qt, 4) + 1) * P
                v.wait_ge(slc_exp, nth(i, n) + 1)
                v.wait_ge(win_exp, nth(i, n) + 1)
                cc = pr[:, CC:CC + NCB]
                step(v.tensor_tensor_reduce(cc, cc, c["seen"][:, qt, :], 1.0, 0.0, ALU.mult, ALU.add, rs[:, m, 2:3]))
                step(v.tensor_scalar(co[:], rs[:, m, :], 1e-30, None, ALU.max))
                step(v.reciprocal(co[:], co[:]))
                step(v.tensor_tensor(co[:], co[:], gst[:, qt, gr, :], ALU.mult))
                for slot, (c0, n_) in enumerate(((0, w), (WC, ww), (CC, NCB))):
                    ins = v.tensor_scalar(pr[:, c0:c0 + n_], pr[:, c0:c0 + n_], co[:, slot:slot + 1], None, ALU.mult)
                    ins.then_inc(v_step, 1)
                    last = cnt.next()
                v.wait_ge(v_step, last)
                v.sem_inc(weighted, 1)

            def output(i, n):
                qt, gr = units[n]
                k = RO.at(f"O{n}", i)
                v.wait_ge(o_filled, k.full)
                rows, cols = slice(gr * DN, (gr + 1) * DN), slice(qt * P, (qt + 1) * P)
                v.tensor_tensor(oBT[rows, ds(i, 1), cols].rearrange("p a n -> p (a n)"), ps[rows, k.bank, 0:P],
                                zh[rows, cols], ALU.mult).then_inc(o_emptied, 1)

            with v.Fori(0, PAIRS) as i:
                cnt = Count(i, 205)

                def step(ins):
                    ins.then_inc(v_step, 1)
                    v.wait_ge(v_step, cnt.next())

                gates = g.gates[:, 0:PT, :].rearrange("p t (g h x) -> p t g h x", g=2, h=4)
                for to, src in ((slice(0, 2), slice(1, 3)), (slice(2, 3), slice(0, 1))):
                    step(v.tensor_copy(gst[:, :, :, to], gates[:, :, :, ds(i, 1), src].rearrange(
                        "p t g a x -> p t g (a x)")))
                v.wait_ge(a_emptied, RA.at("q2", i).done)
                step(v.tensor_copy(g.qS[:, ds(i, 1), :].rearrange("p a n -> p (a n)"), qT[:, SEQ:T]))
                v.wait_ge(z_tanh, i + 1)
                step(v.scalar_tensor_tensor(zh[:], zt[:], 1.0, zh[:], ALU.add, ALU.mult))
                step(v.tensor_copy(g.zS[:, ds(i, 1), :].rearrange("p a n -> p (a n)"), zh[:, SEQ:T]))
                for n in range(NU + 3):
                    if n < NU:
                        maxima(i, n, step)
                    if 1 <= n <= NU:
                        weigh(i, n - 1, step)
                    if n >= 3:
                        output(i, n - 3)
                v.wait_ge(o_emptied, RO.at(f"O{NU - 1}", i).done)
                v.sem_inc(turn_done, 1)
                cnt.end()


def stage_sample(nc, g, caches, page_table, state_win, pos_v, row_consts):
    parts = row_parts()
    ROWS, HALF, NEW = 64, CS * P, SAMPLE
    NM = PAST // CS
    with ExitStack() as outer:
        def sbo(name, shape, dt=F32):
            return outer.enter_context(nc.sbuf_tensor("s_" + name, shape, dt))

        small = {k: v for k, v in parts.items() if k != "before"}
        wc = sum(a.size for a in small.values()) // P
        ctile = sbo("ctile", [P, wc])
        c = Packed(ctile, small)
        big = sbo("big", [P, 4 * HALF + CS * NM + PAST + NEW])
        Z = sbo("Z", [P, NB, P])
        G = [big[:, n * HALF:(n + 1) * HALF] for n in range(4)]
        XTf = big[:, 4 * HALF:4 * HALF + CS * NM]
        XT = XTf.rearrange("p (j m) -> p j m", j=CS)
        srow = big[:, 4 * HALF + CS * NM:]
        idx = sbo("idx", [P, 2 * NB], U32)
        idxk = sbo("idxk", [P, 2], U32)
        idxv = sbo("idxv", [P, 2], U32)
        qblk = sbo("qblk", [P, NB, ROWS])
        qb = sbo("qb", [P, ROWS])
        lq = sbo("lq", [P, NB, ROWS])
        posV = sbo("posV", [P, CS, P])
        Oc = sbo("Oc", [ROWS, NB, P])
        p4 = sbo("p4", [ROWS, NB, SB])
        SEL = sbo("SEL", [ROWS, NB, NBLK])
        gr = sbo("gr", [ROWS, NB, 3])
        passed = outer.enter_context(nc.semaphore("s_passed"))

        with ExitStack() as ctx:
            sem = lambda name: ctx.enter_context(nc.semaphore("s0_" + name))
            pt = ctx.enter_context(nc.sbuf_tensor("s_pt", [P, 2 * NB], I32))
            gt = ctx.enter_context(nc.sbuf_tensor("s_gt", [ROWS, NB, 8, 3], F32))
            blkT = ctx.enter_context(nc.sbuf_tensor("s_blkT", [P, P], F32))
            ps3 = ctx.enter_context(nc.psum_tensor("s0_ps", [P, 3, 512], F32))
            ps = ps3[:, 0, :]
            loaded, filled, blk_ready, v_step = sem("loaded"), sem("filled"), sem("blk_ready"), sem("v_step")
            ALL = 16 * (1 + PAGES // 2 + 4)
            block = ctx.enter_context(nc.Block())

            @block.sync
            def _(sp):
                sp.dma_start(ctile[:], row_consts[:, 0:wc]).then_inc(loaded, 16)
                pages = page_table.rearrange("b (t q) -> q (b t)", t=2)
                with nc.allow_non_contiguous_dma(reason="16 page numbers of four bytes for each partition"):
                    for q in range(PAGES // 2):
                        sp.dma_start(pt[q * 8:(q + 1) * 8, :], pages[q].partition_broadcast(8)
                                     ).then_inc(loaded, 16)
                for x in range(2):
                    for half in range(2):
                        sp.dma_start(posV[x * ROWS:(x + 1) * ROWS, :, half * DN:(half + 1) * DN],
                                     pos_v[0, x * CS:(x + 1) * CS, :].partition_broadcast(ROWS)
                                     ).then_inc(loaded, 16)
                sp.wait_ge(loaded, ALL)

            @block.tensor
            def _(pe):
                pe.transpose(ps3[:, 1, 0:P], g.blk[:, 0, :], g.ident).then_inc(filled, 1)
                pe.wait_ge(loaded, ALL)
                for b in range(NB):
                    ins = pe.matmul(ps[0:ROWS, b * 24:(b + 1) * 24], c["tok_row"][0:SAMPLE, b, :],
                                    g.gates[0:SAMPLE, PT, :], start=True, stop=True)
                ins.then_inc(filled, 1)
                pe.wait_ge(blk_ready, 1)
                pe.matmul(ps3[:, 2, :], blkT[:], qblk[:].rearrange("p b r -> p (b r)"), start=True, stop=True
                          ).then_inc(filled, 1)

            @block.vector
            def _(v):
                n = Count()

                def step(ins):
                    ins.then_inc(v_step, 1)
                    v.wait_ge(v_step, n.next())

                step(v.memset(qblk[:], 0.0))
                for gi in range(2):
                    r = slice(gi * DN, (gi + 1) * DN)
                    for h in range(PAIRS):
                        c0 = gi * 32 + h * NS
                        step(v.tensor_copy(qblk[r, :, c0:c0 + NS], g.qS[r, h, :].rearrange("p (b t) -> p b t", t=NS)))
                v.wait_ge(filled, 1)
                v.tensor_copy(blkT[:], ps3[:, 1, 0:P]).then_inc(blk_ready, 1)
                v.wait_ge(filled, 3)
                step(v.tensor_copy(lq[:].rearrange("p b r -> p (b r)"), ps3[:, 2, :]))
                v.wait_ge(loaded, ALL)
                step(v.tensor_scalar(idx[:], pt[:], 8.0, c["mod8"], ALU.mult, ALU.add))
                step(v.tensor_tensor(gt[:], ps[0:ROWS, 0:NB * 24].rearrange("r (b h x) -> r b h x", b=NB, h=8),
                                     rep(rep(c["pick"][0:ROWS, :], 2, 3), 1, NB), ALU.mult))
                step(v.tensor_reduce(gr[:], gt[:].rearrange("r b h x -> r b x h"), AX, ALU.add))

        def gathers(gp, kinds, idx_tiles, loaded, released, i_sems, passed):
            def gather(x):
                for half in range(2):
                    gp.indirect_dma_start(
                        out=G[2 * x + half], out_offset=None,
                        in_=kinds[x][0].rearrange("n (m j) g d -> (n m) (j g d)", j=CS),
                        in_offset=bass.IndirectOffsetOnAxis(ap=idx_tiles[x][:, half:half + 1], axis=0)
                    ).then_inc(loaded[x], 16)

            def fetch(x, n):
                gp.wait_ge(loaded[x], 32 * n)
                released(x, n - 1)
                gp.sem_inc(passed, 1)
                gp.tensor_copy(idx_tiles[x][:], idx[:, ds(2 * n, 2)]).then_inc(i_sems[x], 1)
                gp.wait_ge(i_sems[x], n + 1)
                gp.sem_inc(passed, 1)
                gather(x)

            for x in range(2):
                gp.tensor_copy(idx_tiles[x][:], idx[:, 0:2]).then_inc(i_sems[x], 1)
                gp.wait_ge(i_sems[x], 1)
                gather(x)
            fetch(0, 1)
            with gp.Fori(0, NB - 2) as i:
                fetch(0, i + 2)
                fetch(1, i + 1)
            fetch(1, NB - 1)

        with ExitStack() as ctx:
            sem = lambda name: ctx.enter_context(nc.semaphore("s1_" + name))
            ps = ctx.enter_context(nc.psum_tensor("s1_ps", [P, 8, 512], F32))
            LQ = srow[:, 0:CS * P].rearrange("p (j x r) -> p j x r", j=CS, x=2)
            PX = srow[:, CS * P:2 * CS * P].rearrange("p (j c) -> p j c", j=CS)
            S2 = ctx.enter_context(nc.sbuf_tensor("s1_S2", [P, NM], F32))
            pw = ctx.enter_context(nc.sbuf_tensor("s1_pw", [ROWS, 1 + NM], F32))
            pc = pw[:, 1:1 + NM]
            pcT = ctx.enter_context(nc.sbuf_tensor("s1_pcT", [P, 2, P], F32))
            nm = ctx.enter_context(nc.sbuf_tensor("s1_nm", [ROWS, 1], F32))
            rs = ctx.enter_context(nc.sbuf_tensor("s1_rs", [ROWS, 1], F32))
            RX = Ring([0, 1, 2], [f"X{n}" for n in range(CS // 2)])
            RA = Ring([3], ["S2"])
            RD = Ring([4, 5, 6, 7], ["sc", "pT"] + [f"V{n}" for n in range(4)])
            x_filled, x_emptied, a_filled, a_emptied, d_filled, d_emptied = (
                sem("x_filled"), sem("x_emptied"), sem("a_filled"), sem("a_emptied"), sem("d_filled"), sem("d_emptied"))
            loaded = [sem("k_loaded"), sem("v_loaded")]
            i_sems = [sem("k_index"), sem("v_index")]
            lq_ready, scaled, exp_done, p_ready, v_step = (
                sem("lq_ready"), sem("scaled"), sem("exp_done"), sem("p_ready"), sem("v_step"))
            block = ctx.enter_context(nc.Block())

            @block.gpsimd
            def _(gp):
                def released(x, i):
                    if x == 0:
                        gp.wait_ge(x_filled, RX.at("X7", i).full)
                    else:
                        gp.wait_ge(d_filled, RD.at("V3", i).full)

                gathers(gp, caches[0:2], (idxk, idxv), loaded, released, i_sems, passed)

            @block.tensor
            def _(pe):
                def turn_keys(i):
                    pe.wait_ge(loaded[0], 32 * i + 32)
                    for n in range(CS // 2):
                        k = RX.at(f"X{n}", i)
                        pe.wait_ge(x_emptied, k.free)
                        for jj in range(2):
                            for half in range(2):
                                j = 2 * n + jj
                                ins = pe.transpose(ps[:, k.bank, (2 * jj + half) * P:(2 * jj + half + 1) * P],
                                                   G[half][:, j * P:(j + 1) * P], g.ident)
                        ins.then_inc(x_filled, 1)

                def sequence(i, more):
                    k = RA.at("S2", i)
                    pe.wait_ge(a_emptied, k.free)
                    pe.wait_ge(lq_ready, i + 1)
                    pe.wait_ge(x_emptied, RX.at("X7", i).done)
                    for j in range(CS):
                        ins = pe.matmul(ps[:, k.bank, 0:NM], LQ[:, j, :, :].rearrange("p x r -> p (x r)"), XT[:, j, :],
                                        start=j == 0, stop=j == CS - 1)
                    ins.then_inc(a_filled, 1)
                    k = RD.at("sc", i)
                    pe.wait_ge(d_emptied, k.free)
                    pe.wait_ge(a_emptied, RA.at("S2", i).done)
                    for x in range(2):
                        ins = pe.matmul(ps[0:ROWS, k.bank, 0:NCS], g.ident[:, x * ROWS:(x + 1) * ROWS],
                                        S2[:, x:x + NCS], start=x == 0, stop=x == 1)
                    ins.then_inc(d_filled, 1)
                    if more:
                        turn_keys(i + 1)
                    k = RD.at("pT", i)
                    pe.wait_ge(d_emptied, k.free)
                    pe.wait_ge(p_ready, i + 1)
                    for half in range(2):
                        for x in range(2):
                            c0 = half * P + 1 - x
                            q = 2 * half + x
                            ins = pe.matmul(ps[:, k.bank, q * ROWS:(q + 1) * ROWS], pw[:, c0:c0 + P],
                                            g.ident[0:ROWS, 0:ROWS], start=True, stop=True)
                    ins.then_inc(d_filled, 1)
                    pe.wait_ge(loaded[1], 32 * i + 32)
                    pe.wait_ge(d_emptied, RD.at("pT", i).done)
                    for n in range(4):
                        k = RD.at(f"V{n}", i)
                        pe.wait_ge(d_emptied, k.free)
                        for half in range(2):
                            ins = pe.matmul(ps[:, k.bank, :], pcT[:, half, :], G[2 + half][:, n * 512:(n + 1) * 512],
                                            start=half == 0, stop=half == 1)
                        ins.then_inc(d_filled, 1)

                turn_keys(0)
                with pe.Fori(0, NB - 1) as i:
                    sequence(i, True)
                sequence(NB - 1, False)

            @block.scalar
            def _(act):
                def evac(i, ns):
                    for n in ns:
                        k = RX.at(f"X{n}", i)
                        act.wait_ge(x_filled, k.full)
                        act.copy(XTf[:, n * 512:(n + 1) * 512], ps[:, k.bank, :]).then_inc(x_emptied, 1)

                def sequence(i, more):
                    k = RA.at("S2", i)
                    act.wait_ge(a_filled, k.full)
                    act.copy(S2[:], ps[:, k.bank, 0:NM]).then_inc(a_emptied, 1)
                    if more:
                        evac(i + 1, range(0, 3))
                    act.wait_ge(scaled, i + 1)
                    act.activation(pc[:, 0:NCS], pc[:, 0:NCS], ACT.Exp, bias=nm[:, 0:1], accum_out=rs[:, 0:1]
                                   ).then_inc(exp_done, 1)
                    if more:
                        evac(i + 1, range(3, CS // 2))

                evac(0, range(CS // 2))
                with act.Fori(0, NB - 1) as i:
                    sequence(i, True)
                sequence(NB - 1, False)

            @block.vector
            def _(v):
                v.sem_inc(x_emptied, 3)
                v.sem_inc(a_emptied, 1)
                v.sem_inc(d_emptied, 4)
                v.memset(pw[:], 0.0).then_inc(v_step, 1)

                def weigh_queries(i):
                    v.tensor_tensor(LQ, rep(rep(lq[:, ds(i, 1), :].rearrange("p a r -> p (a r)"), 1, 2), 1, CS),
                                    rep(g.posT[:, 0, :].rearrange("p (x j) -> p j x", x=2), 3, ROWS), ALU.mult
                                    ).then_inc(lq_ready, 1)

                def sequence(i, more):
                    n_ = Count(i, 4)

                    def step(ins):
                        ins.then_inc(v_step, 1)
                        v.wait_ge(v_step, n_.next() + 1)

                    k = RD.at("sc", i)
                    v.wait_ge(d_filled, k.full)
                    v.tensor_copy(pc[:, 0:NCS], ps[0:ROWS, k.bank, 0:NCS]).then_inc(d_emptied, 1)
                    v.wait_ge(d_emptied, k.done)
                    v.tensor_reduce(nm[:], pc[:, 0:NCS], AX, ALU.max, negate=True).then_inc(scaled, 1)
                    v.wait_ge(exp_done, i + 1)
                    step(v.tensor_scalar(rs[:], rs[:], 1e-30, None, ALU.max))
                    step(v.reciprocal(rs[:], rs[:]))
                    v.tensor_scalar(pc[:, 0:NCS], pc[:, 0:NCS], rs[:, 0:1], None, ALU.mult).then_inc(p_ready, 1)
                    v.wait_ge(p_ready, i + 1)
                    step(v.tensor_reduce(p4[:, ds(i, 1), :].rearrange("r a n -> r (a n)"),
                                         pc.rearrange("r (n c) -> r n c", c=4), AX, ALU.add))
                    k = RD.at("pT", i)
                    v.wait_ge(d_filled, k.full)
                    v.tensor_copy(pcT[:].rearrange("p h r -> p (h r)"), ps[:, k.bank, 0:2 * P]).then_inc(d_emptied, 1)
                    if more:
                        v.wait_ge(a_filled, RA.at("S2", i).full)
                        weigh_queries(i + 1)
                    for n in range(4):
                        k = RD.at(f"V{n}", i)
                        v.wait_ge(d_filled, k.full)
                        v.tensor_tensor(PX[:, 4 * n:4 * n + 4, :], ps[:, k.bank, :].rearrange("p (j c) -> p j c", j=4),
                                        posV[:, 4 * n:4 * n + 4, :], ALU.mult).then_inc(d_emptied, 1)
                    v.wait_ge(d_emptied, RD.at("V3", i).done)
                    step(v.tensor_reduce(Z[:, ds(i, 1), :].rearrange("p a c -> p (a c)"),
                                         PX.rearrange("p j c -> p c j"), AX, ALU.add))
                    n_.end()

                weigh_queries(0)
                with v.Fori(0, NB - 1) as i:
                    sequence(i, True)
                sequence(NB - 1, False)

        with ExitStack() as ctx:
            sem = lambda name: ctx.enter_context(nc.semaphore("s2_" + name))
            ps = ctx.enter_context(nc.psum_tensor("s2_ps", [P, 8, 512], F32))
            ZT = big[:, 3 * NBLK * NBLK:3 * NBLK * NBLK + NB * ROWS].rearrange("p (b r) -> p b r", b=NB)
            z_ready = sem("z_ready")
            NN = NBLK * NBLK
            gt, eq, before = (big[0:ROWS, n * NN:(n + 1) * NN].rearrange("r (i j) -> r i j", i=NBLK) for n in range(3))
            s = ctx.enter_context(nc.sbuf_tensor("s2_s", [ROWS, NBLK], F32))
            rank = ctx.enter_context(nc.sbuf_tensor("s2_rank", [ROWS, NBLK], F32))
            b_loaded, filled, ranked, v_step = sem("b_loaded"), sem("filled"), sem("ranked"), sem("v_step")
            block = ctx.enter_context(nc.Block())

            @block.sync
            def _(sp):
                sp.dma_start(before.rearrange("r i j -> r (i j)"), row_consts[0:ROWS, wc:wc + NN]).then_inc(b_loaded, 16)

            @block.tensor
            def _(pe):
                for b in range(NB):
                    ins = pe.matmul(ps[0:ROWS, 0, 0:SB], c["heads_in"][0:ROWS, b, :], p4[:, b, :],
                                    start=b == 0, stop=b == NB - 1)
                ins.then_inc(filled, 1)
                for b in range(NB):
                    ins = pe.transpose(ps[:, 3 + b // 4, b % 4 * P:(b % 4 + 1) * P], Z[:, b, :], g.ident)
                ins.then_inc(filled, 1)
                pe.wait_ge(z_ready, 1)
                for b in range(NB):
                    ins = pe.matmul(ps[0:ROWS, 5 + b // 4, b % 4 * P:(b % 4 + 1) * P], ZT[:, b, :], g.blk[:, 1, :],
                                    start=True, stop=True)
                ins.then_inc(filled, 1)
                pe.wait_ge(ranked, 1)
                for b in range(NB):
                    ins = pe.matmul(ps[0:ROWS, 1 + b // 4, b % 4 * NBLK:(b % 4 + 1) * NBLK],
                                    c["heads_out"][0:ROWS, b, :], rank[:], start=True, stop=True)
                ins.then_inc(filled, 1)

            @block.vector
            def _(v):
                n = Count()

                def step(ins):
                    ins.then_inc(v_step, 1)
                    v.wait_ge(v_step, n.next())

                v.wait_ge(filled, 2)
                for x in range(2):
                    src = ps[:, 3 + x, :].rearrange("p (b h r) -> p b h r", b=4, h=2)
                    step(v.tensor_copy(ZT[:, 4 * x:4 * x + 4, :], src[:, :, 0, :]))
                    ins = v.tensor_tensor(ZT[:, 4 * x:4 * x + 4, :], src[:, :, 1, :], ZT[:, 4 * x:4 * x + 4, :], ALU.add)
                    if x == 0:
                        step(ins)
                ins.then_inc(z_ready, 1)
                step(v.memset(s[:], 0.0))
                step(v.tensor_copy(s[:, 0:SB], ps[0:ROWS, 0, 0:SB]))
                step(v.tensor_tensor(s[:], s[:], c["force"][0:ROWS, :], ALU.add))
                sj, si = rep(s[:, :], 1, NBLK), rep(s[:, :], 2, NBLK)
                step(v.tensor_tensor(gt, sj, si, ALU.is_gt))
                step(v.tensor_tensor(eq, sj, si, ALU.is_equal))
                v.wait_ge(b_loaded, 16)
                step(v.tensor_tensor(eq, eq, before, ALU.mult))
                step(v.tensor_tensor(gt, gt, eq, ALU.add))
                step(v.tensor_reduce(rank[:], gt, AX, ALU.add))
                v.tensor_scalar(rank[:], rank[:], float(TOP), None, ALU.is_lt).then_inc(ranked, 1)
                v.wait_ge(filled, 3)
                for x in range(2):
                    step(v.tensor_copy(Oc[:, 4 * x:4 * x + 4, :].rearrange("r b e -> r (b e)"), ps[0:ROWS, 5 + x, :]))
                v.wait_ge(filled, 4)
                for x in range(2):
                    step(v.tensor_scalar(SEL[:, 4 * x:4 * x + 4, :].rearrange("r b n -> r (b n)"),
                                         ps[0:ROWS, 1 + x, 0:4 * NBLK], -1.0, BIG, ALU.add, ALU.mult))

        with ExitStack() as ctx:
            sem = lambda name: ctx.enter_context(nc.semaphore("s3_" + name))

            def sb(name, shape, dt=F32):
                return ctx.enter_context(nc.sbuf_tensor("s3_" + name, shape, dt))

            ps = ctx.enter_context(nc.psum_tensor("s3_ps", [P, 8, 512], F32))
            NT = 2 * CS
            pT, pTn = sb("pT", [P, NT, ROWS]), sb("pTn", [NEW, ROWS])
            wT, wpT, wpTn = sb("wT", [P, WIN]), sb("wpT", [P, 4, ROWS]), sb("wpTn", [NEW, ROWS])
            wrow = sb("wrow", [ROWS, WIN + NEW])
            row = srow[0:ROWS, :]
            wk, wv = sb("wk", [P, 4, P]), sb("wv", [P, 4, P])
            selb = sb("selb", [ROWS, 512])
            newb = sb("newb", [ROWS, NEW])
            mx = sb("mx", [ROWS, 9 + 2])
            nm, co = sb("nm", [ROWS, 2]), sb("co", [ROWS, 3])
            rs = sb("rs", [ROWS, 6])
            acc = sb("acc", [ROWS, P])
            trs = sb("trs", [P, PAIRS * NS])
            RX = Ring([0, 1], [f"X{n}" for n in range(CS // 2)] + ["wT"])
            RA = Ring([2], ["P0", "P2"])
            RD = Ring([3, 4, 5, 6, 7], [f"s{n}" for n in range(8)] + ["sn", "ws", "P1", "P3", "wP", "O", "wO", "tr"])
            x_filled, x_emptied, a_filled, a_emptied, d_filled, d_emptied = (
                sem("x_filled"), sem("x_emptied"), sem("a_filled"), sem("a_emptied"), sem("d_filled"), sem("d_emptied"))
            loaded = [sem("k_loaded"), sem("v_loaded")]
            i_sems = [sem("k_index"), sem("v_index")]
            q_parts, taken = sem("q_parts"), sem("taken")
            wk_loaded, wv_loaded, q_ready, maxed, exp_done, acc_ready, o_written, v_step = (
                sem("wk_loaded"), sem("wv_loaded"), sem("q_ready"), sem("maxed"), sem("exp_done"), sem("acc_ready"),
                sem("o_written"), sem("v_step"))
            block = ctx.enter_context(nc.Block())

            @block.sync
            def _(sp):
                def load(x, i):
                    sp.dma_start((wk, wv)[x][:].rearrange("p s n -> p (s n)"), state_win[x][0, ds(i, 1)].rearrange(
                        "a (p s) g d -> (a p) (s g d)", s=4)).then_inc((wk_loaded, wv_loaded)[x], 16)

                load(0, 0)
                load(1, 0)
                sp.wait_ge(x_filled, RX.at("wT", 0).full)
                load(0, 1)
                with sp.Fori(0, NB - 2) as i:
                    sp.wait_ge(x_filled, RX.at("wT", i + 1).full)
                    load(0, i + 2)
                    sp.wait_ge(d_filled, RD.at("wO", i).full)
                    load(1, i + 1)
                sp.wait_ge(d_filled, RD.at("wO", NB - 2).full)
                load(1, NB - 1)

            @block.gpsimd
            def _(gp):
                def released(x, i):
                    if x == 0:
                        gp.wait_ge(x_filled, RX.at("X7", i).full)
                    else:
                        gp.wait_ge(d_filled, RD.at("O", i).full)

                gathers(gp, caches[2:4], (idxk, idxv), loaded, released, i_sems, passed)

            @block.tensor
            def _(pe):
                def turn_keys(i):
                    pe.wait_ge(loaded[0], 32 * i + 32)
                    for n in range(CS // 2):
                        k = RX.at(f"X{n}", i)
                        pe.wait_ge(x_emptied, k.free)
                        for jj in range(2):
                            for half in range(2):
                                j = 2 * n + jj
                                ins = pe.transpose(ps[:, k.bank, (2 * jj + half) * P:(2 * jj + half + 1) * P],
                                                   G[half][:, j * P:(j + 1) * P], g.ident)
                        ins.then_inc(x_filled, 1)
                    k = RX.at("wT", i)
                    pe.wait_ge(x_emptied, k.free)
                    pe.wait_ge(wk_loaded, 16 * i + 16)
                    for s in range(4):
                        ins = pe.transpose(ps[:, k.bank, s * P:(s + 1) * P], wk[:, s, :], g.ident)
                    ins.then_inc(x_filled, 1)

                def scores(i):
                    pe.wait_ge(q_ready, i + 1)
                    pe.wait_ge(x_emptied, RX.at("X7", i).done)
                    for n in range(8):
                        k = RD.at(f"s{n}", i)
                        pe.wait_ge(d_emptied, k.free)
                        pe.matmul(ps[0:ROWS, k.bank, :], qb[:], XTf[:, n * 512:(n + 1) * 512], start=True, stop=True
                                  ).then_inc(d_filled, 1)
                    k = RD.at("sn", i)
                    pe.wait_ge(d_emptied, k.free)
                    pe.matmul(ps[0:ROWS, k.bank, 0:NEW], qb[:], g.slcS[:], start=True, stop=True)
                    pe.matmul(ps[0:ROWS, k.bank, NEW:2 * NEW], qb[:], g.winS[:], start=True, stop=True
                              ).then_inc(d_filled, 1)
                    k = RD.at("ws", i)
                    pe.wait_ge(d_emptied, k.free)
                    pe.wait_ge(x_emptied, RX.at("wT", i).done)
                    pe.matmul(ps[0:ROWS, k.bank, :], qb[:], wT[:], start=True, stop=True).then_inc(d_filled, 1)

                def turn(i, n):
                    R, filled, emptied = (RD, d_filled, d_emptied) if n % 2 else (RA, a_filled, a_emptied)
                    k = R.at(f"P{n}", i)
                    pe.wait_ge(emptied, k.free)
                    pe.wait_ge(exp_done, 5 * i + n + 1)
                    for q in range(8):
                        to, part = ps[:, k.bank, q * ROWS:(q + 1) * ROWS], row[:, (8 * n + q) * P:(8 * n + q + 1) * P]
                        if q == 0:
                            ins = pe.matmul(to, part, g.ident[0:ROWS, 0:ROWS], start=True, stop=True)
                        else:
                            ins = pe.transpose(to, part, g.ident[0:ROWS, 0:ROWS])
                    ins.then_inc(filled, 1)

                def turn_window(i):
                    k = RD.at("wP", i)
                    pe.wait_ge(d_emptied, k.free)
                    pe.wait_ge(exp_done, 5 * i + 5)
                    for s in range(4):
                        pe.matmul(ps[:, k.bank, s * ROWS:(s + 1) * ROWS], wrow[:, s * P:(s + 1) * P],
                                  g.ident[0:ROWS, 0:ROWS], start=True, stop=True)
                    pe.matmul(ps[0:NEW, k.bank, 256:320], row[:, PAST:PAST + NEW], g.ident[0:ROWS, 0:ROWS],
                              start=True, stop=True)
                    pe.matmul(ps[0:NEW, k.bank, 320:384], wrow[:, WIN:WIN + NEW], g.ident[0:ROWS, 0:ROWS],
                              start=True, stop=True).then_inc(d_filled, 1)

                def values(i, n):
                    k = RD.at("O", i)
                    if n == 0:
                        pe.wait_ge(d_emptied, k.free)
                        pe.wait_ge(loaded[1], 32 * i + 32)
                    R, emptied = (RD, d_emptied) if n % 2 else (RA, a_emptied)
                    pe.wait_ge(emptied, R.at(f"P{n}", i).done)
                    for t in range(8 * n, 8 * n + 8):
                        j, half = t // 2, t % 2
                        pe.matmul(ps[0:ROWS, k.bank, 0:P], pT[:, t, :], G[2 + half][:, j * P:(j + 1) * P],
                                  start=t == 0, stop=False)

                def sequence(i, more):
                    scores(i)
                    if more:
                        turn_keys(i + 1)
                    turn(i, 0)
                    turn(i, 1)
                    values(i, 0)
                    turn(i, 2)
                    values(i, 1)
                    turn(i, 3)
                    values(i, 2)
                    turn_window(i)
                    values(i, 3)
                    pe.wait_ge(d_emptied, RD.at("wP", i).done)
                    pe.matmul(ps[0:ROWS, RD.at("O", i).bank, 0:P], pTn[:], g.vS[:, 0, :], start=False, stop=True
                              ).then_inc(d_filled, 1)
                    k = RD.at("wO", i)
                    pe.wait_ge(d_emptied, k.free)
                    pe.wait_ge(wv_loaded, 16 * i + 16)
                    for s in range(4):
                        pe.matmul(ps[0:ROWS, k.bank, 0:P], wpT[:, s, :], wv[:, s, :], start=s == 0, stop=False)
                    pe.matmul(ps[0:ROWS, k.bank, 0:P], wpTn[:], g.vS[:, 1, :], start=False, stop=True
                              ).then_inc(d_filled, 1)
                    k = RD.at("tr", i)
                    pe.wait_ge(d_emptied, k.free)
                    pe.wait_ge(acc_ready, i + 1)
                    pe.matmul(ps[:, k.bank, 0:ROWS], acc[:], g.ident[0:ROWS, 0:ROWS], start=True, stop=True
                              ).then_inc(d_filled, 1)

                turn_keys(0)
                with pe.Fori(0, NB - 1) as i:
                    sequence(i, True)
                sequence(NB - 1, False)

            @block.scalar
            def _(act):
                def evac(i, names):
                    for name in names:
                        k = RX.at(name, i)
                        to = wT[:] if name == "wT" else XTf[:, int(name[1]) * 512:(int(name[1]) + 1) * 512]
                        act.wait_ge(x_filled, k.full)
                        act.copy(to, ps[:, k.bank, :]).then_inc(x_emptied, 1)

                def exps(i, n):
                    if n == 0:
                        act.wait_ge(maxed, 2 * i + 1)
                    part = row[:, n * PAST // 4:(n + 1) * PAST // 4]
                    act.activation(part, part, ACT.Exp, bias=nm[:, 0:1], accum_out=rs[:, n:n + 1]).then_inc(exp_done, 1)

                def sequence(i, more):
                    shares = (["X0", "X1", "X2"], ["X3", "X4"], ["X5", "X6"], ["X7", "wT"])
                    for n, share in enumerate(shares):
                        if more:
                            evac(i + 1, share)
                        exps(i, n)
                    act.wait_ge(maxed, 2 * i + 2)
                    part = row[:, PAST:PAST + NEW]
                    act.activation(part, part, ACT.Exp, bias=nm[:, 0:1], accum_out=rs[:, 4:5])
                    act.activation(wrow[:], wrow[:], ACT.Exp, bias=nm[:, 1:2], accum_out=rs[:, 5:6]).then_inc(exp_done, 1)
                    for n in (0, 2):
                        k = RA.at(f"P{n}", i)
                        act.wait_ge(a_filled, k.full)
                        act.copy(pT[:, 8 * n:8 * n + 8, :].rearrange("p t r -> p (t r)"), ps[:, k.bank, :]
                                 ).then_inc(a_emptied, 1)

                evac(0, [f"X{n}" for n in range(8)] + ["wT"])
                with act.Fori(0, NB - 1) as i:
                    sequence(i, True)
                sequence(NB - 1, False)

            @block.vector
            def _(v):
                v.sem_inc(x_emptied, 2)
                v.sem_inc(a_emptied, 1)
                v.sem_inc(d_emptied, 5)

                def prepare(i):
                    one = ds(i, 1)
                    v.tensor_copy(selb[:].rearrange("r (j b c) -> r j b c", j=2, c=4),
                                  rep(rep(SEL[:, one, 0:SB].rearrange("r a n -> r (a n)"), 2, 4), 1, 2)
                                  ).then_inc(q_parts, 1)
                    v.tensor_copy(newb[:], c["new"][0:ROWS, one, :].rearrange("r a n -> r (a n)")).then_inc(q_parts, 1)
                    v.tensor_copy(qb[:], qblk[:, one, :].rearrange("p a r -> p (a r)")).then_inc(q_ready, 1)

                def masked(i, to, scores, mask, at):
                    return v.tensor_tensor_reduce(to, scores, mask, 1.0, -BIG, ALU.add, ALU.max, mx[:, at:at + 1])

                def sequence(i, more):
                    n_ = Count(i, 9)

                    def step(ins):
                        ins.then_inc(v_step, 1)
                        v.wait_ge(v_step, n_.next())

                    one = ds(i, 1)
                    v.wait_ge(q_parts, 2 * i + 2)
                    for n in range(8):
                        k = RD.at(f"s{n}", i)
                        v.wait_ge(d_filled, k.full)
                        v.sem_inc(taken, 1)
                        masked(i, row[:, n * 512:(n + 1) * 512], ps[0:ROWS, k.bank, :], selb[:], n
                               ).then_inc(d_emptied, 1)
                    k = RD.at("sn", i)
                    v.wait_ge(d_filled, k.full)
                    v.sem_inc(taken, 1)
                    step(masked(i, row[:, PAST:PAST + NEW], ps[0:ROWS, k.bank, 0:NEW], newb[:], 8))
                    v.sem_inc(taken, 1)
                    masked(i, wrow[:, WIN:WIN + NEW], ps[0:ROWS, k.bank, NEW:2 * NEW], newb[:], 9).then_inc(d_emptied, 1)
                    v.wait_ge(d_emptied, k.done)
                    v.tensor_reduce(nm[:, 0:1], mx[:, 0:9], AX, ALU.max, negate=True).then_inc(maxed, 1)
                    k = RD.at("ws", i)
                    v.wait_ge(d_filled, k.full)
                    v.sem_inc(taken, 1)
                    masked(i, wrow[:, 0:WIN], ps[0:ROWS, k.bank, :], c["win"][0:ROWS].rearrange("r s p -> r (s p)"), 10
                           ).then_inc(d_emptied, 1)
                    v.wait_ge(d_emptied, k.done)
                    v.tensor_reduce(nm[:, 1:2], mx[:, 9:11], AX, ALU.max, negate=True).then_inc(maxed, 1)
                    if more:
                        prepare(i + 1)
                    step(v.tensor_copy(co[:], gr[:, one, :].rearrange("r a n -> r (a n)")))
                    step(v.tensor_scalar(acc[:], Oc[:, one, :].rearrange("r a e -> r (a e)"), co[:, 0:1], None, ALU.mult))
                    for n in (1, 3):
                        k = RD.at(f"P{n}", i)
                        v.wait_ge(d_filled, k.full)
                        v.tensor_copy(pT[:, 8 * n:8 * n + 8, :].rearrange("p t r -> p (t r)"), ps[:, k.bank, :]
                                      ).then_inc(d_emptied, 1)
                    k = RD.at("wP", i)
                    v.wait_ge(d_filled, k.full)
                    step(v.tensor_copy(wpT[:].rearrange("p t r -> p (t r)"), ps[:, k.bank, 0:256]))
                    step(v.tensor_copy(pTn[:], ps[0:NEW, k.bank, 256:320]))
                    v.tensor_copy(wpTn[:], ps[0:NEW, k.bank, 320:384]).then_inc(d_emptied, 1)
                    v.wait_ge(exp_done, 5 * i + 5)
                    step(v.tensor_reduce(rs[:, 4:5], rs[:, 0:5], AX, ALU.add))
                    step(v.reciprocal(rs[:, 4:6], rs[:, 4:6]))
                    step(v.tensor_tensor(co[:, 1:3], co[:, 1:3], rs[:, 4:6], ALU.mult))
                    for n, name in enumerate(("O", "wO")):
                        k = RD.at(name, i)
                        v.wait_ge(d_filled, k.full)
                        v.scalar_tensor_tensor(acc[:], ps[0:ROWS, k.bank, 0:P], co[:, n + 1:n + 2], acc[:], ALU.mult,
                                               ALU.add).then_inc(d_emptied, 1)
                        v.wait_ge(d_emptied, k.done)
                    v.tensor_tensor(acc[:], acc[:], c["own"][0:ROWS, :], ALU.mult).then_inc(acc_ready, 1)
                    k = RD.at("tr", i)
                    v.wait_ge(d_filled, k.full)
                    step(v.tensor_copy(trs[:], ps[:, k.bank, 0:PAIRS * NS]))
                    v.tensor_tensor(trs[:], ps[:, k.bank, 32:32 + PAIRS * NS], trs[:], ALU.add).then_inc(d_emptied, 1)
                    v.wait_ge(d_emptied, k.done)
                    v.tensor_tensor(g.oBT[:, :, ds(SEQ + i * NS, NS)], trs[:].rearrange("p (h t) -> p h t", h=PAIRS),
                                    g.zS[:, :, ds(i * NS, NS)], ALU.mult).then_inc(o_written, 1)
                    v.wait_ge(o_written, i + 1)
                    n_.end()

                prepare(0)
                with v.Fori(0, NB - 1) as i:
                    sequence(i, True)
                sequence(NB - 1, False)


def stage_merge(nc, g, x_prompt, x_sample, w_in, w_branches, w_out, final_gain, y_prompt, y_sample):
    hT, oAT, oBT = g.hT, g.oAT, g.oBT
    units = [(par, s) for par in range(2) for s in range(len(THIRDS))]
    NU = len(units)
    RG = Ring([0, 1, 2, 3], [f"g{n}{x}" for n in range(NU) for x in range(2)])
    RB = Ring([4, 5, 6, 7], [f"b{n}{x}" for n in range(NU) for x in range(2)])
    TURNS = KT // 2
    with ExitStack() as ctx:
        def sb(name, shape, dt=F32):
            return ctx.enter_context(nc.sbuf_tensor("m_" + name, shape, dt))

        def sem(name):
            return ctx.enter_context(nc.semaphore("m_" + name))

        Wg = [sb(f"Wg{n}", [P, 2, KT, P]) for n in range(2)]
        Wa = [sb(f"Wa{n}", [P, KT, P]) for n in range(2)]
        Wb = [sb(f"Wb{n}", [P, PAIRS, P]) for n in range(2)]
        Wo = sb("Wo", [P, KT, D])
        mixed = sb("mixed", [P, KT, T])
        sg = [[sb(f"sg{n}{x}", [P, 512]) for x in range(2)] for n in range(2)]
        NX = 3
        xt = [sb(f"xt{n}", [P, D]) for n in range(NX)]
        gain, junk = sb("gain", [P, D]), sb("junk", [P, D])
        ss, rstd, half = sb("ss", [P, TT]), sb("rstd", [P, TT]), sb("half", [P, 1])
        ps = ctx.enter_context(nc.psum_tensor("m_ps", [P, 8, 512], F32))
        w_loaded = [sem(f"w_loaded{n}") for n in range(2)]
        wo_loaded, gain_loaded = sem("wo_loaded"), sem("gain_loaded")
        x_loaded = [sem(f"x_loaded{n}") for n in range(NX)]
        y_stored = [sem(f"y_stored{n}") for n in range(NX)]
        g_filled, g_emptied, b_filled, b_emptied = (
            sem("g_filled"), sem("g_emptied"), sem("b_filled"), sem("b_emptied"))
        mixes, o_filled = sem("mixes"), sem("o_filled")
        summed, squared, rooted, p_step, y_ready = (
            sem("summed"), sem("squared"), sem("rooted"), sem("p_step"), sem("y_ready"))
        block = ctx.enter_context(nc.Block())
        w_rows = w_in[0].rearrange("(k p) n -> p k n", p=P)
        wa_rows = w_branches[0][0].rearrange("(k p) n -> p k n", p=P)
        wb_rows = w_branches[1][0].rearrange("(g r p) n -> g p r n", g=2, p=DN)

        def x_tile(prompt, sample, t):
            if t < PT:
                return prompt[0, t * P:(t + 1) * P, :]
            return sample.rearrange("b s n -> (b s) n")

        def rows(t):
            return P if t < PT else SAMPLE

        @block.sync
        def _(sp):
            def load(par, col):
                cols = ds(col, P)
                for x in range(2):
                    sp.dma_start(Wg[par][:, x, :, :], w_rows[:, :, ds(C_M + x * D + col, P)]
                                 ).then_inc(w_loaded[par], 16)
                sp.dma_start(Wa[par][:], wa_rows[:, :, cols]).then_inc(w_loaded[par], 16)
                for gr in range(2):
                    sp.dma_start(Wb[par][gr * DN:(gr + 1) * DN], wb_rows[gr][:, :, cols]).then_inc(w_loaded[par], 16)

            for par in range(2):
                load(par, par * P)
            sp.dma_start(Wo[:], w_out[0].rearrange("(k p) n -> p k n", p=P)).then_inc(wo_loaded, 16)
            sp.dma_start(gain[:], final_gain.partition_broadcast(P)).then_inc(gain_loaded, 16)
            for t in range(NX):
                sp.dma_start(xt[t][:], x_tile(x_prompt, x_sample, t)).then_inc(x_loaded[t], 16)
            with sp.Fori(0, TURNS - 1) as i:
                for par in range(2):
                    n = par * len(THIRDS) + len(THIRDS) - 1
                    sp.wait_ge(g_filled, RG.at(f"g{n}1", i).full)
                    sp.wait_ge(b_filled, RB.at(f"b{n}1", i).full)
                    load(par, (2 * i + par + 2) * P)
            for t in range(TT):
                r = rows(t)
                sp.wait_ge(y_ready, t + 1)
                sp.dma_start(x_tile(y_prompt, y_sample, t), xt[t % NX][0:r]).then_inc(y_stored[t % NX], 16)
                if t + NX < TT:
                    sp.wait_ge(y_stored[t % NX], 16 * (t // NX + 1))
                    sp.dma_start(xt[t % NX][0:rows(t + NX)], x_tile(x_prompt, x_sample, t + NX)
                                 ).then_inc(x_loaded[t % NX], 16)
            for n in range(NX):
                sp.wait_ge(y_stored[n], 16 * len(range(n, TT, NX)))

        @block.tensor
        def _(pe):
            with pe.Fori(0, TURNS) as i:
                for n, (par, s) in enumerate(units):
                    t0, w = THIRDS[s]
                    if s == 0:
                        pe.wait_ge(w_loaded[par], 16 * 5 * i + 16 * 5)
                    for x in range(2):
                        k = RG.at(f"g{n}{x}", i)
                        pe.wait_ge(g_emptied, k.free)
                        for kt in range(KT):
                            ins = pe.matmul(ps[:, k.bank, 0:w], Wg[par][:, x, kt, :], hT[:, kt, t0:t0 + w],
                                            start=kt == 0, stop=kt == KT - 1)
                        ins.then_inc(g_filled, 1)
                    for x, (W, src, depth) in enumerate(((Wa, oAT, KT), (Wb, oBT, PAIRS))):
                        k = RB.at(f"b{n}{x}", i)
                        pe.wait_ge(b_emptied, k.free)
                        for kt in range(depth):
                            ins = pe.matmul(ps[:, k.bank, 0:w], W[par][:, kt, :], src[:, kt, t0:t0 + w],
                                            start=kt == 0, stop=kt == depth - 1)
                        ins.then_inc(b_filled, 1)
            pe.wait_ge(wo_loaded, 16)
            pe.wait_ge(mixes, TURNS * NU + 2)
            for t in range(TT):
                r = rows(t)
                for h in range(2):
                    n = 2 * t + h
                    if n >= 8:
                        pe.wait_ge(summed, n - 7)
                    for kt in range(KT):
                        ins = pe.matmul(ps[0:r, n % 8, :], mixed[:, kt, t * P:t * P + r],
                                        Wo[:, kt, h * 512:(h + 1) * 512], start=kt == 0, stop=kt == KT - 1)
                    ins.then_inc(o_filled, 1)

        @block.scalar
        def _(act):
            with act.Fori(0, TURNS) as i:
                for n, (par, s) in enumerate(units):
                    w = THIRDS[s][1]
                    act.wait_ge(mixes, i * NU + n + 1)
                    for x in range(2):
                        k = RG.at(f"g{n}{x}", i)
                        act.wait_ge(g_filled, k.full)
                        act.activation(sg[n % 2][x][:, 0:w], ps[:, k.bank, 0:w], ACT.Tanh, scale=0.5
                                       ).then_inc(g_emptied, 1)
            for t in range(TT):
                r = rows(t)
                act.wait_ge(summed, 2 * t + 2)
                if t:
                    act.wait_ge(squared, t)
                act.activation(junk[0:r], xt[t % NX][0:r], ACT.Square, accum_out=ss[0:r, t:t + 1]).then_inc(squared, 1)

        @block.gpsimd
        def _(gp):
            gp.memset(half[:], -0.5).then_inc(p_step, 1)
            gp.wait_ge(p_step, 1)
            for t in range(TT):
                r = rows(t)
                gp.wait_ge(squared, t + 1)
                gp.tensor_scalar(rstd[0:r, t:t + 1], ss[0:r, t:t + 1], 1.0 / D, EPS, ALU.mult, ALU.add
                                 ).then_inc(p_step, 1)
                gp.wait_ge(p_step, t + 2)
                gp.tensor_tensor(rstd[0:r, t:t + 1], rstd[0:r, t:t + 1], half[0:r], ALU.pow).then_inc(rooted, 1)

        @block.vector
        def _(v):
            v.sem_inc(g_emptied, 4)
            v.sem_inc(b_emptied, 4)
            v.sem_inc(mixes, 2)
            with v.Fori(0, TURNS) as i:
                for n, (par, s) in enumerate(units):
                    t0, w = THIRDS[s]
                    ts = [sg[n % 2][x][:, 0:w] for x in range(2)]
                    for x in range(2):
                        k = RB.at(f"b{n}{x}", i)
                        v.wait_ge(g_emptied, RG.at(f"g{n}{x}", i).done)
                        v.wait_ge(b_filled, k.full)
                        v.scalar_tensor_tensor(ts[x], ts[x], 1.0, ps[:, k.bank, 0:w], ALU.add, ALU.mult
                                               ).then_inc(b_emptied, 1)
                    v.wait_ge(b_emptied, k.done)
                    v.tensor_tensor(mixed[:, ds(2 * i + par, 1), t0:t0 + w].rearrange("p a n -> p (a n)"), ts[0], ts[1],
                                    ALU.add).then_inc(mixes, 1)
            v.wait_ge(gain_loaded, 16)
            for t in range(TT + 1):
                if t < TT:
                    r = rows(t)
                    v.wait_ge(x_loaded[t % NX], 16 * (t // NX + 1))
                    for h in range(2):
                        n = 2 * t + h
                        to = xt[t % NX][0:r, h * 512:(h + 1) * 512]
                        v.wait_ge(o_filled, n + 1)
                        v.scalar_tensor_tensor(to, ps[0:r, n % 8, :], 0.5, to, ALU.mult, ALU.add
                                               ).then_inc(summed, 1)
                if t:
                    r = rows(t - 1)
                    y = xt[(t - 1) % NX][0:r]
                    v.wait_ge(rooted, t)
                    v.scalar_tensor_tensor(y, y, rstd[0:r, t - 1:t], gain[0:r], ALU.mult, ALU.mult
                                           ).then_inc(y_ready, 1)

class Globals:
    pass


def build(nc, ins, outs):
    (x_prompt, x_sample, cache_k_cmp, cache_v_cmp, cache_k_slc, cache_v_slc, state_win_k, state_win_v,
     state_conv, state_gdn, page_table, norm_gain, w_in, conv_w, a_log, dt_bias, gdn_gain,
     cmp_pos_k, cmp_w_k, cmp_pos_v, cmp_w_v, w_branch_a, w_branch_b, w_out, final_gain,
     consts, nsa_consts, row_consts) = ins
    (y_prompt, y_sample, k_cmp_p, v_cmp_p, k_slc_p, v_slc_p, win_k_p, win_v_p, conv_p, gdn_p,
     k_cmp_s, v_cmp_s, k_slc_s, v_slc_s, win_k_s, win_v_s, conv_s, gdn_s) = outs
    g = Globals()
    with ExitStack() as ctx:
        def sb(name, shape, dt=F32):
            return ctx.enter_context(nc.sbuf_tensor(name, shape, dt))

        g.hT = sb("hT", [P, KT, T])
        g.oAT = sb("oAT", [P, HEADS, T])
        g.gates = sb("gates", [P, TT, 24])
        g.ident_tile = sb("identity", [P, P])
        g.ident = g.ident_tile[:, :]
        with ExitStack() as first:
            parts = const_parts()
            width = sum(a.size for a in parts.values()) // P
            g.ctile = first.enter_context(nc.sbuf_tensor("consts", [P, width], F32))
            g.consts = consts
            g.c = Packed(g.ctile, parts)
            g.beta = first.enter_context(nc.sbuf_tensor("beta", [P, TT, HEADS], F32))
            g.SC = first.enter_context(nc.sbuf_tensor("SC", [P, HEADS, 6, TT], F32))
            g.DEC = first.enter_context(nc.sbuf_tensor("DEC", [P, HEADS, 2 * PT], F32))
            g.taps = first.enter_context(nc.sbuf_tensor("taps", [P, HEADS, 3, CONV], F32))
            stage_norm(nc, g, x_prompt, x_sample, norm_gain, w_in, conv_w, a_log, dt_bias)
            stage_gdn(nc, g, w_in, state_conv, state_gdn, gdn_gain, conv_p, conv_s, gdn_p, gdn_s)
        g.oBT = sb("oBT", [P, PAIRS, T])
        with ExitStack() as third:
            def sb3(name, shape):
                return third.enter_context(nc.sbuf_tensor(name, shape, F32))

            g.posT = sb3("posT", [P, 2, CL])
            g.blk = sb3("blk", [P, 2, P])
            g.vS = sb3("vS", [SAMPLE, 2, P])
            g.qS = sb3("qS", [P, PAIRS, SAMPLE])
            g.zS = sb3("zS", [P, PAIRS, SAMPLE])
            g.slcS = sb3("slcS", [P, SAMPLE])
            g.winS = sb3("winS", [P, SAMPLE])
            with ExitStack() as second:
                def sb2(name, shape):
                    return second.enter_context(nc.sbuf_tensor(name, shape, F32))

                g.KV = sb2("KV", [P, TT, 6 * P])
                g.slcT = sb2("slcT", [P, T])
                g.winT = sb2("winT", [P, T])
                g.kcT = sb2("kcT", [P, NCB])
                g.vc = sb2("vc", [NCB, P])
                g.Wpair = sb2("Wpair", [P, 2, KT, P])
                stage_kv(nc, g, w_in, (cmp_pos_k, cmp_pos_v), (cmp_w_k, cmp_w_v), (state_win_k, state_win_v),
                         (k_cmp_p, v_cmp_p, k_slc_p, v_slc_p, win_k_p, win_v_p), (k_cmp_s, v_cmp_s, k_slc_s, v_slc_s),
                         (win_k_s, win_v_s))
                stage_prompt(nc, g, w_in, nsa_consts)
            stage_sample(nc, g, (cache_k_cmp, cache_v_cmp, cache_k_slc, cache_v_slc), page_table,
                         (state_win_k, state_win_v), cmp_pos_v, row_consts)
        stage_merge(nc, g, x_prompt, x_sample, w_in, (w_branch_a, w_branch_b), w_out, final_gain, y_prompt, y_sample)


_INS = ['x_prompt', 'x_sample', 'cache_k_cmp', 'cache_v_cmp', 'cache_k_slc', 'cache_v_slc', 'state_win_k',
        'state_win_v', 'state_conv', 'state_gdn', 'page_table', 'norm_gain', 'w_in', 'conv_w', 'a_log', 'dt_bias',
        'gdn_gain', 'cmp_pos_k', 'cmp_w_k', 'cmp_pos_v', 'cmp_w_v', 'w_branch_a', 'w_branch_b', 'w_out', 'final_gain']
_KV = (2, 64)
_OUTS = ([(1, SEQ, D), (NB, NS, D)] + [(1, 1, SEQ) + _KV] * 4 + [(1, 1, WIN) + _KV] * 2
         + [(1, 1, 3, 3072), (1, 1, HEADS, P, P)] + [(1, NB, NS) + _KV] * 4 + [(1, NB, WIN) + _KV] * 2
         + [(1, NB, 3, 3072), (1, NB, HEADS, P, P)])


def kernel(**inputs):
    import numpy as _np
    import concourse.bacc as _bacc
    from concourse import mybir as _mybir
    from concourse.bass_utils import run_bass_kernel_spmd as _run

    nc = _bacc.Bacc("TRN2", target_bir_lowering=False, num_devices=1)
    arrays, args, outs = {}, [], []
    given = {name: _np.ascontiguousarray(inputs[name]) for name in _INS}
    given["consts"] = pack(const_parts())
    given["nsa_consts"] = pack(nsa_parts())
    given["row_consts"] = pack(row_parts())
    for name, a in given.items():
        arrays[f"in_{name}_dram"] = a
        args.append(nc.dram_tensor(f"in_{name}_dram", a.shape, _mybir.dt.from_np(a.dtype), kind="ExternalInput").ap())
    for i, shape in enumerate(_OUTS):
        outs.append(nc.dram_tensor(f"out_{i}_dram", shape, _mybir.dt.float32, kind="ExternalOutput").ap())
    build(nc, args, outs)
    r = _run(nc, [arrays], core_ids=[0])
    return tuple(r.results[0][f"out_{i}_dram"] for i in range(len(_OUTS)))
```
